# Optimizing a Trainium2 kernel written in Bass

```python
import math
import jax, jax.numpy as jnp
from jax import lax
import numpy as np

"""Two-layer hybrid bidirectional encoder trunk (parallel head groups: QK-normed GQA with 2-D axial rotary + short gated convolution mixer; ConvFFN gated MLP; Gemma-3n style per-layer input embeddings) applied with the SAME weights to two request groups.

Inputs:
  x_prompt (BATCH, SEQ, D_MODEL), x_sample (DEC_BATCH, DEC_SEQ, D_MODEL)
  p_prompt (DEPTH, BATCH, SEQ, PLE_DIM), p_sample (DEPTH, DEC_BATCH, DEC_SEQ, PLE_DIM)
  per-layer weights stacked along a leading DEPTH axis.
Outputs: (y_prompt (BATCH, SEQ, D_MODEL), y_sample (DEC_BATCH, DEC_SEQ, D_MODEL)).
"""

D_MODEL = 1024
BATCH = 1
SEQ = 512
DEPTH = 2
DEC_BATCH = 1
DEC_SEQ = 256
PAST_LEN = 128

GRID_W = 64
HEAD_DIM = 64
N_HEADS = 8
N_KV_HEADS = 2
Q_PER_KV = N_HEADS // N_KV_HEADS
ATTN_W = N_HEADS * HEAD_DIM
KV_W = N_KV_HEADS * HEAD_DIM
CONV_W = 512
MIX_W = ATTN_W + CONV_W
D_IN = ATTN_W + 2 * KV_W + 3 * CONV_W
SPLITS = (ATTN_W, ATTN_W + KV_W, ATTN_W + 2 * KV_W, ATTN_W + 2 * KV_W + CONV_W, ATTN_W + 2 * KV_W + 2 * CONV_W)
D_FF = 2816
CONV_K = 3
PLE_DIM = 256
Q_BLOCK = 128
ROPE_THETA = 10000.0
EPS = 1e-6

kernel_name = "hybrid_bidir_attn_shortconv_encoder"

def rmsnorm(x, g):
    xf = x.astype(jnp.float32)
    y = xf * lax.rsqrt(jnp.mean(xf * xf, axis=-1, keepdims=True) + EPS) * g.astype(jnp.float32)
    return y.astype(x.dtype)

def dwconv3(x, w):
    xp = jnp.pad(x, ((0, 0), (1, 1), (0, 0)))
    return xp[:, :-2] * w[0] + xp[:, 1:-1] * w[1] + xp[:, 2:] * w[2]

def axial_rope_tables(seq_len):
    rows = seq_len // GRID_W
    row = jnp.repeat(jnp.arange(rows), GRID_W).astype(jnp.float32)
    col = jnp.tile(jnp.arange(GRID_W), rows).astype(jnp.float32)
    half = HEAD_DIM // 2
    freqs = ROPE_THETA ** (-jnp.arange(0, half, 2, dtype=jnp.float32) / half)
    ang_r = row[:, None] * freqs[None, :]
    ang_c = col[:, None] * freqs[None, :]
    ang = jnp.concatenate([ang_r, ang_r, ang_c, ang_c], axis=-1)
    return jnp.cos(ang), jnp.sin(ang)

def apply_axial_rope(x, cos, sin):
    q4 = HEAD_DIM // 4
    x1, x2, x3, x4 = x[..., :q4], x[..., q4:2 * q4], x[..., 2 * q4:3 * q4], x[..., 3 * q4:]
    rot = jnp.concatenate([-x2, x1, -x4, x3], axis=-1)
    c = cos[None, :, None, :].astype(x.dtype)
    s = sin[None, :, None, :].astype(x.dtype)
    return x * c + rot * s

def bidir_gqa(q, k, v):
    B, S = q.shape[0], q.shape[1]
    nb = S // Q_BLOCK
    scale = 1.0 / math.sqrt(HEAD_DIM)
    qb = q.reshape(B, nb, Q_BLOCK, N_KV_HEADS, Q_PER_KV, HEAD_DIM).transpose(1, 0, 2, 3, 4, 5)

    def block(qi):
        s = jnp.einsum('bqkgd,bskd->bkgqs', qi, k).astype(jnp.float32) * scale
        p = jax.nn.softmax(s, axis=-1).astype(v.dtype)
        return jnp.einsum('bkgqs,bskd->bqkgd', p, v)

    o = lax.map(block, qb)
    return o.transpose(1, 0, 2, 3, 4, 5).reshape(B, S, ATTN_W)

def trunk(x, p, attn_norm_g, w_in, q_norm_g, k_norm_g, mix_conv_w, attn_out_g, conv_out_g,
          w_out, ffn_norm_g, w_up, ffn_conv_w, w_down, w_ple_gate, w_ple_proj):
    B, S, _ = x.shape
    cos, sin = axial_rope_tables(S)
    h = x
    for i in range(DEPTH):
        a = rmsnorm(h, attn_norm_g[i])
        z = a @ w_in[i]
        q, k, v, gb, gc, u = jnp.split(z, SPLITS, axis=-1)
        q = q.reshape(B, S, N_HEADS, HEAD_DIM)
        k = k.reshape(B, S, N_KV_HEADS, HEAD_DIM)
        v = v.reshape(B, S, N_KV_HEADS, HEAD_DIM)
        q = apply_axial_rope(rmsnorm(q, q_norm_g[i]), cos, sin)
        k = apply_axial_rope(rmsnorm(k, k_norm_g[i]), cos, sin)
        o_attn = bidir_gqa(q, k, v)
        o_conv = gb * dwconv3(gc * u, mix_conv_w[i])
        mixed = jnp.concatenate([rmsnorm(o_attn, attn_out_g[i]), rmsnorm(o_conv, conv_out_g[i])], axis=-1)
        h = h + mixed @ w_out[i]
        f = dwconv3(rmsnorm(h, ffn_norm_g[i]) @ w_up[i], ffn_conv_w[i])
        g, up = jnp.split(f, 2, axis=-1)
        h = h + (jax.nn.silu(g) * up) @ w_down[i]
        h = h + jax.nn.sigmoid(h @ w_ple_gate[i]) * (p[i] @ w_ple_proj[i])
    return h

def setup_inputs(seed: int = 0) -> dict:
    key = jax.random.key(seed)
    ks = jax.random.split(key, 20)
    f32 = jnp.float32

    def nrm(k, shape, scale):
        return jax.random.normal(k, shape, f32) * scale

    def gain(k, shape):
        return 1.0 + 0.01 * jax.random.normal(k, shape, f32)

    return {
        "x_prompt": nrm(ks[0], (BATCH, SEQ, D_MODEL), 1.0),
        "x_sample": nrm(ks[1], (DEC_BATCH, DEC_SEQ, D_MODEL), 1.0),
        "p_prompt": nrm(ks[2], (DEPTH, BATCH, SEQ, PLE_DIM), 1.0),
        "p_sample": nrm(ks[3], (DEPTH, DEC_BATCH, DEC_SEQ, PLE_DIM), 1.0),
        "attn_norm_g": gain(ks[4], (DEPTH, D_MODEL)),
        "w_in": nrm(ks[5], (DEPTH, D_MODEL, D_IN), D_MODEL ** -0.5),
        "q_norm_g": gain(ks[6], (DEPTH, HEAD_DIM)),
        "k_norm_g": gain(ks[7], (DEPTH, HEAD_DIM)),
        "mix_conv_w": nrm(ks[8], (DEPTH, CONV_K, CONV_W), CONV_K ** -0.5),
        "attn_out_g": gain(ks[9], (DEPTH, ATTN_W)),
        "conv_out_g": gain(ks[10], (DEPTH, CONV_W)),
        "w_out": nrm(ks[11], (DEPTH, MIX_W, D_MODEL), MIX_W ** -0.5),
        "ffn_norm_g": gain(ks[12], (DEPTH, D_MODEL)),
        "w_up": nrm(ks[13], (DEPTH, D_MODEL, 2 * D_FF), D_MODEL ** -0.5),
        "ffn_conv_w": nrm(ks[14], (DEPTH, CONV_K, 2 * D_FF), CONV_K ** -0.5),
        "w_down": nrm(ks[15], (DEPTH, D_FF, D_MODEL), D_FF ** -0.5),
        "w_ple_gate": nrm(ks[16], (DEPTH, D_MODEL, D_MODEL), D_MODEL ** -0.5),
        "w_ple_proj": nrm(ks[17], (DEPTH, PLE_DIM, D_MODEL), PLE_DIM ** -0.5),
    }

def reference(x_prompt, x_sample, p_prompt, p_sample, attn_norm_g, w_in, q_norm_g, k_norm_g,
              mix_conv_w, attn_out_g, conv_out_g, w_out, ffn_norm_g, w_up, ffn_conv_w, w_down,
              w_ple_gate, w_ple_proj):
    y_prompt = trunk(x_prompt, p_prompt, attn_norm_g, w_in, q_norm_g, k_norm_g, mix_conv_w,
                     attn_out_g, conv_out_g, w_out, ffn_norm_g, w_up, ffn_conv_w, w_down,
                     w_ple_gate, w_ple_proj)
    y_sample = trunk(x_sample, p_sample, attn_norm_g, w_in, q_norm_g, k_norm_g, mix_conv_w,
                     attn_out_g, conv_out_g, w_out, ffn_norm_g, w_up, ffn_conv_w, w_down,
                     w_ple_gate, w_ple_proj)
    return (y_prompt, y_sample)


_drawn_inputs = setup_inputs


def setup_inputs(seed=0):
    import zlib

    import numpy as np

    out = dict(_drawn_inputs(seed))
    spreads = {}
    factors = {'attn_norm_g': 3.318,
     'q_norm_g': 8.0,
     'k_norm_g': 8.0,
     'attn_out_g': 22.32,
     'conv_out_g': 23.52,
     'ffn_norm_g': 7.98}
    for name, (base, spread) in spreads.items():
        noise = np.random.default_rng([zlib.crc32(name.encode()), seed]).standard_normal(out[name].shape)
        drawn = base * np.exp(spread * noise) if base else spread * noise
        out[name] = __import__('jax').numpy.asarray(drawn.astype(out[name].dtype))
    for name, factor in factors.items():
        out[name] = (out[name] * factor).astype(out[name].dtype)
    return out
```

```python
from contextlib import ExitStack

import numpy as np

import concourse.bass as bass
from concourse import mybir

F32 = mybir.dt.float32
F32R = mybir.dt.float32r
ALU = mybir.AluOpType
ACT = mybir.ActivationFunctionType
AX_X = mybir.AxisListType.X

P = 128
DEPTH, D_MODEL, SEQ, DEC_SEQ = 2, 1024, 512, 256
T = SEQ + DEC_SEQ
HEAD_DIM, N_HEADS, N_KV = 64, 8, 2
Q_PER_KV = N_HEADS // N_KV
ATTN_W, CONV_W, D_FF, PLE_DIM = 512, 512, 2816, 256
D_IN = ATTN_W + 2 * N_KV * HEAD_DIM + 3 * CONV_W
GRID_W, ROPE_THETA, EPS = 64, 10000.0, 1e-6
SCALE = HEAD_DIM ** -0.5

KT = D_MODEL // P
IN_TILES = D_IN // P
FF_TILES = D_FF // P
HALVES = 2
HALF = FF_TILES // HALVES
KT_PLE = PLE_DIM // P
CHUNKS = ((0, SEQ), (SEQ, T))

UW = T + 4
CW = T + 2
U_PROMPT, U_SAMPLE = slice(1, 1 + SEQ), slice(SEQ + 3, SEQ + 3 + DEC_SEQ)
C_PROMPT, C_SAMPLE = slice(0, SEQ), slice(SEQ + 2, CW)
PADS = (slice(0, 1), slice(SEQ + 1, SEQ + 3), slice(UW - 1, UW))

TILE_K, TILE_V, TILE_GB, TILE_GC, TILE_U = 4, 5, 6, 10, 14
QKV_ORDER = [TILE_K, TILE_V, 0, 1, 2, 3]

ROPE_ORDER = [16 * b + i for b in (0, 2, 1, 3) for i in range(16)]

N_A = 3 + 8 + 4 + HALVES * (HALF + 4) + 8
N_B = 3 + 4 + 4 + HALVES * (HALF + 4) + 8
A_QKV, A_ATT, A_OUT = 0, 3, 11
B_QKV, B_ATT, B_OUT = 0, 3, 7
A_UP = [15, 15 + HALF + 4]
B_UP = [11, 11 + HALF + 4]
A_DOWN, B_DOWN = [a + HALF for a in A_UP], [b + HALF for b in B_UP]
A_PLE, B_PLE = N_A - 8, N_B - 8

V_ATTN, V_FFN, V_MIX, V_QG, V_KG, V_MCONV = 0, 8, 16, 24, 25, 26
V_FCONV = V_MCONV + 3 * 4
N_VEC = V_FCONV + 3 * 2 * FF_TILES

UNITS = ((0, 0, SEQ), (256, 0, SEQ), (SEQ, SEQ, DEC_SEQ))
UQ = 256
N_UNITS = N_HEADS * len(UNITS)


class Event:

    def __init__(self, sem, per_layer, by=1):
        self.sem, self.per_layer, self.by = sem, per_layer, by

    def done(self, layer, k):
        return (layer * self.per_layer + k + 2) * self.by

    def open(self, eng):
        eng.sem_inc(self.sem, self.by)


def trunk_program(nc, x, p, w_in, w_out, w_up, w_down, w_gate, w_proj, vec, tables, mats, y):
    with ExitStack() as ctx:
        def sb(name, shape, dt=F32, where=ctx):
            return where.enter_context(nc.sbuf_tensor(name, shape, dt))

        def event(name, per_layer, by=1):
            return Event(ctx.enter_context(nc.semaphore(name)), per_layer, by)

        h = sb("h", [P, KT, T])
        in_hi, in_lo = sb("in_hi", [P, KT, T], F32R), sb("in_lo", [P, KT, T], F32R)
        raw = {s: sb(f"raw{s}", [P, HALF * P]) for s in "AB"}
        w_hi = {s: sb(f"w_hi{s}", [P, HALF, P], F32R) for s in "AB"}
        w_lo = {s: sb(f"w_lo{s}", [P, HALF, P], F32R) for s in "AB"}
        mix = sb("mix", [P, KT, T])
        mix_flat = mix[:].rearrange("p k t -> p (k t)")
        conv_in, conv_out = sb("conv_in", [P, UW]), sb("conv_out", [P, CW])
        cos_sin = sb("cos_sin", [P, 2, T])
        r_in, r_attn, r_conv = sb("r_in", [P, T]), sb("r_attn", [P, T]), sb("r_conv", [P, T])
        sum_h = sb("sum_h", [P, T])
        mat = sb("mat", [P, 3, P])
        ident, ones, head_ones = mat[:, 0, :], mat[:, 1, :], mat[:, 2, :]
        vc = sb("vc", [P, N_VEC])
        eps = sb("eps", [P, 1])
        top, neg_top, total, inv_total = (sb(n, [P, 4]) for n in ("top", "neg_top", "total", "inv_total"))
        with ExitStack() as att:
            q_st = sb("q_st", [P, N_HEADS, T], F32R, att)
            k_hi, k_lo = sb("k_hi", [P, N_KV, T], F32R, att), sb("k_lo", [P, N_KV, T], F32R, att)
            v_hl = sb("v_hl", [P, T // P, N_KV, 2 * HEAD_DIM], F32R, att)
            sum_c, sq = sb("sum_c", [P, T], F32, att), sb("sq", [P, T], F32, att)
            with ExitStack() as units:
                pt_hi = sb("pt_hi", [P, SEQ // P, UQ], F32R, units)
                pt_lo = sb("pt_lo", [P, SEQ // P, UQ], F32R, units)
                probs = sb("probs", [P, 2, 2, SEQ], F32, units)
                o_low = sb("o_low", [HEAD_DIM, UQ], F32, units)
            z = [sb(f"z{i}", [P, T], F32, att) for i in range(2)]
            zsq, zrot = sb("zsq", [P, T], F32, att), sb("zrot", [P, T], F32, att)
            qk_hi, qk_lo = sb("qk_hi", [P, T], F32R, att), sb("qk_lo", [P, T], F32R, att)
        with ExitStack() as ffn:
            act_hi, act_lo = sb("act_hi", [P, HALF, CW], F32R, ffn), sb("act_lo", [P, HALF, CW], F32R, ffn)
        with ExitStack() as ple:
            sb("ple_pad", [P, 12 * 1024], F32, ple)
            p_hi, p_lo = sb("p_hi", [P, KT_PLE, T], F32R, ple), sb("p_lo", [P, KT_PLE, T], F32R, ple)
        zcos = conv_out
        up_in = [mix_flat[:, i * UW:(i + 1) * UW] for i in range(2)]
        up_out = [mix_flat[:, 2 * UW + i * CW:2 * UW + (i + 1) * CW] for i in range(2)]
        p_raw = mix_flat[:, 2 * UW + 2 * CW:2 * UW + 2 * CW + KT_PLE * T]

        ps = {n: ctx.enter_context(nc.psum_tensor(f"ps{n}", [P, 1024], F32)) for n in "ABCD"}

        per = {"A": N_A, "B": N_B}
        raw_in = {s: event(f"raw_in_{s}", per[s], 16) for s in "AB"}
        hi_made = {s: event(f"hi_made_{s}", per[s]) for s in "AB"}
        lo_made = {s: event(f"lo_made_{s}", per[s]) for s in "AB"}
        job_done = {s: event(f"job_done_{s}", per[s]) for s in "AB"}
        emptied = {s: event(f"emptied_{s}", per[s]) for s in "AB"}
        vec_set = event("vec_set", 1, 16)
        in_hi_made, in_lo_made = event("in_hi_made", 4 * KT), event("in_lo_made", 4 * KT)
        h_done = event("h_done", 4 * KT)
        squared, summed = event("squared", 24), event("summed", 28)
        stat_ps, stat_root, stat_ready = event("stat_ps", 4), event("stat_root", 4), event("stat_ready", 4)
        z_sq, z_ss, z_root = event("z_sq", 5), event("z_ss", 5), event("z_root", 5)
        z_inv, z_scaled = event("z_inv", 5), event("z_scaled", 5)
        z_swapped = event("z_swapped", 20, 16)
        z_cos, z_sin, z_roped = event("z_cos", 5), event("z_sin", 5), event("z_roped", 5)
        z_hi, z_lo = event("z_hi", 5), event("z_lo", 5)
        qk_placed = event("qk_placed", 8 + 4 * 4, 16)
        v_turned, v_hi, v_lo = event("v_turned", 1), event("v_hi", 1), event("v_lo", 1)
        padded = event("padded", 2)
        gated, centre, left, right, mixed = (event(n, 4) for n in ("gated", "centre", "left", "right", "mixed"))
        nq = 2 * N_UNITS
        scored, topped, neg_topped, exped = (event(n, nq) for n in ("scored", "topped", "neg_topped", "exped"))
        inverted, normed, turned, pt_hi_made, pt_lo_made = (
            event(n, nq) for n in ("inverted", "normed", "turned", "pt_hi_made", "pt_lo_made"))
        weighed, o_low_out, o_out = (event(n, N_UNITS) for n in ("weighed", "o_low_out", "o_out"))
        scaled = {"conv": event("scaled_conv", 8), "attn": event("scaled_attn", 8)}
        added = event("added", 8)
        up_centre = [event(f"up_centre{i}", FF_TILES) for i in range(2)]
        up_left = [event(f"up_left{i}", FF_TILES) for i in range(2)]
        up_right = [event(f"up_right{i}", FF_TILES) for i in range(2)]
        silued, product = event("silued", FF_TILES), event("product", FF_TILES)
        act_hi_made, act_lo_made = event("act_hi_made", FF_TILES), event("act_lo_made", FF_TILES)
        p_in, p_hi_made, p_lo_made = event("p_in", 1, 16), event("p_hi_made", 1), event("p_lo_made", 1)
        sigmoided, gated_p = event("sigmoided", 8), event("gated_p", 8)
        const_in = ctx.enter_context(nc.semaphore("const_in"))
        x_in = ctx.enter_context(nc.semaphore("x_in"))
        eps_set = ctx.enter_context(nc.semaphore("eps_set"))
        first_sq = ctx.enter_context(nc.semaphore("first_sq"))
        y_out = ctx.enter_context(nc.semaphore("y_out"))

        settled = {e: ctx.enter_context(nc.semaphore(f"settled_{e}")) for e in ("pool", "dve", "sp")}

        def unit_of(n):
            return (n // 3,) + UNITS[n % 3]

        block = ctx.enter_context(nc.Block())

        @block.sync
        def _(sp):
            for e in (*raw_in.values(), vec_set, z_swapped, qk_placed, p_in):
                e.open(sp)
            sp.dma_start(mat[:], mats).then_inc(const_in, 16)
            sp.dma_start(cos_sin[:], tables).then_inc(const_in, 16)
            sp.dma_start(h[:, 0:4, :], x[:, 0:4, :]).then_inc(x_in, 16)
            sp.dma_start(h[:, 4:8, :], x[:, 4:8, :]).then_inc(x_in, 16)

            def load(s, l, k, src, kt):
                w, tile = src
                at = sp.snap(tile)
                sp.wait_ge(lo_made[s].sem, lo_made[s].done(l, k - 1))
                sp.dma_start(raw[s][:, 0:kt * P], w[at]).then_inc(raw_in[s].sem, 16)

            def swap(l, r):
                sp.wait_ge(z_scaled.sem, z_scaled.done(l, r))
                sp.sem_inc(settled["sp"], 1)
                sp.wait_ge(z_roped.sem, z_roped.done(l, r - 1))
                for to, of in ((0, 32), (32, 0), (64, 96), (96, 64)):
                    sp.dma_start(zrot[to:to + 32, :], z[r % 2][of:of + 32, :]).then_inc(z_swapped.sem, 16)

            def place_k(l):
                sp.wait_ge(z_lo.sem, z_lo.done(l, 0))
                for g in range(N_KV):
                    for half in range(2):
                        rows = slice(half * 64, half * 64 + 64)
                        for dst, src in ((k_hi, qk_hi), (k_lo, qk_lo)):
                            sp.dma_start(dst[rows, g, :].bitcast(F32), src[g * 64:g * 64 + 64, :].bitcast(F32)).then_inc(qk_placed.sem, 16)

            def place_q(l, j):
                sp.wait_ge(z_lo.sem, z_lo.done(l, j + 1))
                for hh in range(2):
                    for half, src in enumerate((qk_hi, qk_lo)):
                        sp.dma_start(q_st[half * 64:half * 64 + 64, 2 * j + hh, :].bitcast(F32),
                                     src[hh * 64:hh * 64 + 64, :].bitcast(F32)).then_inc(qk_placed.sem, 16)

            with sp.Fori(0, DEPTH) as l:
                def w_in_load(s, k, tile):
                    load(s, l, k, (w_in, l * IN_TILES + tile), KT)

                layer = sp.snap(l)
                sp.wait_ge(act_lo_made.sem, act_lo_made.done(l, -1))
                sp.dma_start(vc[:], vec[layer]).then_inc(vec_set.sem, 16)
                for n in range(4):
                    w_in_load("AB"[n % 2], n // 2, QKV_ORDER[n])
                w_in_load("A", 2, QKV_ORDER[4])
                swap(l, 0)
                place_k(l)
                w_in_load("B", 2, QKV_ORDER[5])
                w_in_load("A", A_ATT, TILE_GB)
                swap(l, 1)
                place_q(l, 0)
                w_in_load("B", B_ATT, TILE_GC)
                for j in range(1, 4):
                    swap(l, j + 1)
                    place_q(l, j)
                for j in range(4):
                    w_in_load("A", A_ATT + 2 * j + 1, TILE_U + j)
                    if j < 3:
                        w_in_load("A", A_ATT + 2 * j + 2, TILE_GB + j + 1)
                        w_in_load("B", B_ATT + j + 1, TILE_GC + j + 1)
                with sp.Fori(0, 4) as i:
                    load("A", l, A_OUT + i, (w_out, l * 8 + 2 * i), KT)
                    load("B", l, B_OUT + i, (w_out, l * 8 + 2 * i + 1), KT)
                layer = sp.snap(l)
                sp.wait_ge(in_lo_made.sem, in_lo_made.done(l, 2 * KT - 1))
                sp.dma_start(p_raw, p[layer]).then_inc(p_in.sem, 16)
                for f in range(HALVES):
                    with sp.Fori(0, HALF) as i:
                        load("A", l, A_UP[f] + i, (w_up, l * 2 * FF_TILES + f * HALF + i), KT)
                        load("B", l, B_UP[f] + i, (w_up, l * 2 * FF_TILES + FF_TILES + f * HALF + i), KT)
                    with sp.Fori(0, 4) as i:
                        load("A", l, A_DOWN[f] + i, (w_down, (l * HALVES + f) * 8 + 2 * i), HALF)
                        load("B", l, B_DOWN[f] + i, (w_down, (l * HALVES + f) * 8 + 2 * i + 1), HALF)
                with sp.Fori(0, 8) as i:
                    load("A", l, A_PLE + i, (w_gate, l * 8 + i), KT)
                    load("B", l, B_PLE + i, (w_proj, l * 8 + i), KT_PLE)
            for m in range(KT):
                sp.wait_ge(h_done.sem, h_done.done(DEPTH - 1, 3 * KT + m))
                sp.dma_start(y[:, m, :], h[:, m, :]).then_inc(y_out, 16)
            sp.wait_ge(y_out, 16 * KT)

        @block.tensor
        def _(pe):
            for e in (*job_done.values(), stat_ps, z_ss, v_turned, scored, turned, weighed):
                e.open(pe)
            pe.wait_ge(const_in, 32)

            def ready(s, l, k):
                pe.wait_ge(lo_made[s].sem, lo_made[s].done(l, k))
                pe.wait_ge(emptied[s].sem, emptied[s].done(l, k - 1))

            def piece(s, kt, out, hi, lo, first, last):
                mm = None
                for n, (w, a) in enumerate(((w_hi[s], hi), (w_hi[s], lo), (w_lo[s], hi))):
                    for (c0, c1), cols in zip(CHUNKS, a):
                        mm = nc.tensor.matmul(ps[out][:, c0:c1], w[:, kt, :], cols,
                                              start=first and n == 0, stop=last and n == 2)
                return mm

            def cols(t, kt):
                return t[:, kt, 0:SEQ], t[:, kt, SEQ:T]

            def act_cols(t, kt):
                return t[:, kt, C_PROMPT], t[:, kt, C_SAMPLE]

            def in_piece(s, kt, out=None, first=None, last=None):
                return piece(s, kt, out or s, cols(in_hi, kt), cols(in_lo, kt),
                             kt == 0 if first is None else first, kt == KT - 1 if last is None else last)

            def in_job(s, l, k, phase=None):
                ready(s, l, k)
                for kt in range(KT):
                    if phase is not None:
                        pe.wait_ge(in_lo_made.sem, in_lo_made.done(l, phase * KT + kt))
                    mm = in_piece(s, kt)
                mm.then_inc(job_done[s].sem, 1)

            def stat(l, n, out, sums, w=ones):
                for c0, c1 in CHUNKS:
                    mm = nc.tensor.matmul(ps[out][:, c0:c1], w, sums[:, c0:c1], start=True, stop=True)
                return mm

            def head_squares(l, r):
                pe.wait_ge(z_sq.sem, z_sq.done(l, r))
                pe.wait_ge(z_root.sem, z_root.done(l, r - 1))
                stat(l, r, "C", zsq, head_ones).then_inc(z_ss.sem, 1)

            def turn_v(l):
                pe.wait_ge(emptied["B"].sem, emptied["B"].done(l, B_QKV))
                for t in range(T // P):
                    mm = nc.tensor.transpose(ps["D"][:, t * P:(t + 1) * P], z[1][:, t * P:(t + 1) * P], ident)
                mm.then_inc(v_turned.sem, 1)

            def scores(l, n):
                head, q0, k0, nk = unit_of(n)
                if n % 6 == 0:
                    pe.wait_ge(qk_placed.sem, qk_placed.done(l, 8 + 4 * (n // 6 + 1) - 1))
                for t in range(2):
                    pe.wait_ge(exped.sem, exped.done(l, 2 * (n - 1) + t))
                    q = q_st[:, head, q0 + t * P:q0 + (t + 1) * P]
                    out = ps["C"][:, t * 512:t * 512 + nk]
                    nc.tensor.matmul(out, q, k_hi[:, head // Q_PER_KV, k0:k0 + nk], start=True, stop=False)
                    nc.tensor.matmul(out, q, k_lo[:, head // Q_PER_KV, k0:k0 + nk], start=False,
                                     stop=True).then_inc(scored.sem, 1)

            def turn(l, n, t):
                nk = unit_of(n)[3]
                pe.wait_ge(normed.sem, normed.done(l, 2 * n + t))
                pe.wait_ge(pt_lo_made.sem, pt_lo_made.done(l, 2 * n + t - 1))
                for b in range(nk // P):
                    mm = nc.tensor.transpose(ps["D"][:, b * P:(b + 1) * P],
                                             probs[:, n % 2, t, b * P:(b + 1) * P], ident)
                mm.then_inc(turned.sem, 1)

            def weigh(l, n):
                head, _, k0, nk = unit_of(n)
                pe.wait_ge(pt_lo_made.sem, pt_lo_made.done(l, 2 * n + 1))
                pe.wait_ge(o_out.sem, o_out.done(l, n - 1))
                nb = nk // P
                for b in range(nb):
                    v = v_hl[:, k0 // P + b, head // Q_PER_KV, :]
                    nc.tensor.matmul(ps["D"][:, 512:512 + UQ], v, pt_hi[:, b, :], start=b == 0, stop=False)
                    mm = nc.tensor.matmul(ps["D"][:, 512:512 + UQ], v, pt_lo[:, b, :], start=False,
                                          stop=b == nb - 1)
                mm.then_inc(weighed.sem, 1)

            with pe.Fori(0, DEPTH) as l:
                in_job("A", l, 0, phase=0)
                pe.wait_ge(summed.sem, summed.done(l, -1))
                stat(l, 0, "C", sum_h).then_inc(stat_ps.sem, 1)
                in_job("B", l, 0)
                pe.wait_ge(stat_root.sem, stat_root.done(l, 0))
                head_squares(l, 0)
                in_job("A", l, 1)
                turn_v(l)
                in_job("B", l, 1)
                head_squares(l, 1)
                in_job("A", l, 2)
                head_squares(l, 2)
                in_job("B", l, 2)
                head_squares(l, 3)

                ready("A", l, A_ATT)
                for kt in range(KT):
                    mm = in_piece("A", kt)
                    if kt == 3:
                        head_squares(l, 4)
                mm.then_inc(job_done["A"].sem, 1)
                pe.wait_ge(z_root.sem, z_root.done(l, 4))
                pe.wait_ge(v_lo.sem, v_lo.done(l, 0))
                pieces = []
                for j in range(4):
                    for s, k in (("A", A_ATT + 2 * j), ("B", B_ATT + j), ("A", A_ATT + 2 * j + 1)):
                        if (s, k) != ("A", A_ATT):
                            pieces += [(s, k, kt) for kt in range(KT)]
                left_over = iter(pieces)

                def next_piece():
                    s, k, kt = next(left_over, (None, None, None))
                    if s:
                        if kt == 0:
                            ready(s, l, k)
                        mm = in_piece(s, kt)
                        if kt == KT - 1:
                            mm.then_inc(job_done[s].sem, 1)

                scores(l, 0)
                for n in range(N_UNITS):
                    next_piece()
                    if n + 1 < N_UNITS:
                        scores(l, n + 1)
                    next_piece()
                    turn(l, n, 0)
                    next_piece()
                    turn(l, n, 1)
                    next_piece()
                    weigh(l, n)

                pe.wait_ge(summed.sem, summed.done(l, 8))
                pe.wait_ge(pt_lo_made.sem, pt_lo_made.done(l, 2 * N_UNITS - 1))
                pe.wait_ge(o_out.sem, o_out.done(l, N_UNITS - 1))
                stat(l, 2, "D", sum_c).then_inc(stat_ps.sem, 1)
                pe.wait_ge(summed.sem, summed.done(l, 9))
                pe.wait_ge(exped.sem, exped.done(l, 2 * N_UNITS - 1))
                stat(l, 1, "C", sum_h).then_inc(stat_ps.sem, 1)
                pe.wait_ge(emptied["B"].sem, emptied["B"].done(l, B_OUT - 1))

                def out_job(s, k, first=False):
                    ready(s, l, k)
                    attn_ps, conv_ps = ("A", "B") if s == "A" else ("C", "D")
                    for n, kt in enumerate((4, 5, 6, 7, 0, 1, 2, 3)):
                        if first:
                            pe.wait_ge(in_lo_made.sem, in_lo_made.done(l, KT + n))
                        mm = in_piece(s, kt, out=conv_ps if kt >= 4 else attn_ps, first=kt % 4 == 0,
                                      last=kt % 4 == 3)
                    mm.then_inc(job_done[s].sem, 1)

                out_job("A", A_OUT, first=True)
                pe.wait_ge(stat_root.sem, stat_root.done(l, 2))
                out_job("B", B_OUT)
                with pe.Fori(1, 4) as i:
                    out_job("A", A_OUT + i)
                    out_job("B", B_OUT + i)

                for f in range(HALVES):
                    if f == 0:
                        in_job("A", l, A_UP[0], phase=2)
                        pe.wait_ge(summed.sem, summed.done(l, 18))
                        pe.wait_ge(emptied["B"].sem, emptied["B"].done(l, B_OUT + 3))
                        stat(l, 3, "C", sum_h).then_inc(stat_ps.sem, 1)
                        in_job("B", l, B_UP[0])
                    with pe.Fori(1 if f == 0 else 0, HALF) as i:
                        in_job("A", l, A_UP[f] + i)
                        in_job("B", l, B_UP[f] + i)
                    def down_job(s, k, first=False):
                        ready(s, l, k)
                        for kt in range(HALF):
                            if first:
                                pe.wait_ge(act_lo_made.sem, act_lo_made.done(l, f * HALF + kt))
                            mm = piece(s, kt, s, act_cols(act_hi, kt), act_cols(act_lo, kt), kt == 0, kt == HALF - 1)
                        mm.then_inc(job_done[s].sem, 1)

                    down_job("A", A_DOWN[f], first=True)
                    down_job("B", B_DOWN[f])
                    with pe.Fori(1, 4) as i:
                        down_job("A", A_DOWN[f] + i)
                        down_job("B", B_DOWN[f] + i)

                def proj_job(k):
                    ready("B", l, k)
                    for kt in range(KT_PLE):
                        mm = piece("B", kt, "B", cols(p_hi, kt), cols(p_lo, kt), kt == 0, kt == KT_PLE - 1)
                    mm.then_inc(job_done["B"].sem, 1)

                in_job("A", l, A_PLE, phase=3)
                pe.wait_ge(p_lo_made.sem, p_lo_made.done(l, 0))
                proj_job(B_PLE)
                with pe.Fori(1, 8) as i:
                    in_job("A", l, A_PLE + i)
                    proj_job(B_PLE + i)

        @block.scalar
        def _(act):
            for e in (*hi_made.values(), in_hi_made, stat_root, z_root, z_hi, v_hi, centre, exped, pt_hi_made,
                      o_low_out, *up_centre, silued, act_hi_made, p_hi_made, sigmoided):
                e.open(act)
            act.wait_ge(eps_set, 1)

            def w_high(s, l, k, kt):
                act.wait_ge(raw_in[s].sem, raw_in[s].done(l, k))
                act.wait_ge(job_done[s].sem, job_done[s].done(l, k - 1))
                nc.scalar.copy(w_hi[s][:, 0:kt, :].rearrange("p k n -> p (k n)"),
                               raw[s][:, 0:kt * P]).then_inc(hi_made[s].sem, 1)

            def root(out, src, n):
                return nc.scalar.activation(out, src, ACT.Sqrt, bias=eps[:, 0:1], scale=1.0 / n)

            def z_roots(l, r):
                act.wait_ge(z_ss.sem, z_ss.done(l, r))
                root(zsq[:], ps["C"][:, 0:T], HEAD_DIM).then_inc(z_root.sem, 1)

            def z_high(l, r):
                act.wait_ge(z_roped.sem, z_roped.done(l, r))
                act.wait_ge(qk_placed.sem, qk_placed.done(l, (8 + 4 * (r - 1) if r else 0) - 1))
                nc.scalar.copy(qk_hi[:], zcos[:, 0:T]).then_inc(z_hi.sem, 1)

            with act.Fori(0, DEPTH) as l:
                w_high("A", l, 0, KT)
                act.wait_ge(vec_set.sem, vec_set.done(l, 0))
                act.wait_ge(h_done.sem, h_done.done(l, -1))
                act.wait_ge(job_done["A"].sem, job_done["A"].done(l, -1))
                for t in range(KT):
                    nc.scalar.activation(in_hi[:, t, :], h[:, t, :], ACT.Copy,
                                         scale=vc[:, V_ATTN + t:V_ATTN + t + 1]).then_inc(in_hi_made.sem, 1)
                    if t == 1:
                        w_high("B", l, 0, KT)
                w_high("A", l, 1, KT)
                act.wait_ge(stat_ps.sem, stat_ps.done(l, 0))
                root(r_in[:], ps["C"][:, 0:T], D_MODEL).then_inc(stat_root.sem, 1)
                w_high("B", l, 1, KT)
                z_roots(l, 0)
                w_high("A", l, 2, KT)
                z_high(l, 0)
                act.wait_ge(v_turned.sem, v_turned.done(l, 0))
                nc.scalar.copy(v_hl[:, :, :, 0:64],
                               ps["D"][:, 0:T].rearrange("p (t g d) -> p t g d", g=N_KV, d=HEAD_DIM)
                               ).then_inc(v_hi.sem, 1)
                w_high("B", l, 2, KT)
                z_roots(l, 1)
                w_high("A", l, A_ATT, KT)
                z_high(l, 1)
                z_roots(l, 2)
                w_high("B", l, B_ATT, KT)
                z_high(l, 2)
                z_roots(l, 3)
                z_high(l, 3)
                z_roots(l, 4)
                z_high(l, 4)
                w_high("A", l, A_ATT + 1, KT)

                def exp(n, t):
                    nk = unit_of(n)[3]
                    act.wait_ge(neg_topped.sem, neg_topped.done(l, 2 * n + t))
                    if n >= 2:
                        act.wait_ge(turned.sem, turned.done(l, 2 * (n - 2) + t))
                    c = 2 * (n % 2) + t
                    nc.scalar.activation(probs[:, n % 2, t, 0:nk], ps["C"][:, t * 512:t * 512 + nk], ACT.Exp,
                                         bias=neg_top[:, c:c + 1], scale=SCALE,
                                         accum_out=total[:, c:c + 1]).then_inc(exped.sem, 1)

                def pt_high(n, t):
                    nb = unit_of(n)[3] // P
                    act.wait_ge(turned.sem, turned.done(l, 2 * n + t))
                    act.wait_ge(weighed.sem, weighed.done(l, n - 1))
                    nc.scalar.copy(pt_hi[:, 0:nb, t * P:(t + 1) * P],
                                   ps["D"][:, 0:nb * P].rearrange("p (b q) -> p b q", q=P)
                                   ).then_inc(pt_hi_made.sem, 1)

                def mixer_centre(j):
                    act.wait_ge(gated.sem, gated.done(l, j))
                    nc.scalar.activation(conv_out[:], conv_in[:, 1:1 + CW], ACT.Copy,
                                         scale=vc[:, V_MCONV + 4 + j:V_MCONV + 5 + j]).then_inc(centre.sem, 1)

                act.wait_ge(z_lo.sem, z_lo.done(l, 4))
                act.wait_ge(qk_placed.sem, qk_placed.done(l, 23))
                exp(0, 0)
                exp(0, 1)
                for n in range(N_UNITS):
                    if n + 1 < N_UNITS:
                        exp(n + 1, 0)
                    pt_high(n, 0)
                    if n + 1 < N_UNITS:
                        exp(n + 1, 1)
                    pt_high(n, 1)
                    act.wait_ge(weighed.sem, weighed.done(l, n))
                    act.wait_ge(o_out.sem, o_out.done(l, n - 1))
                    nc.scalar.copy(o_low[:], ps["D"][64:128, 512:512 + UQ]).then_inc(o_low_out.sem, 1)
                    j, at = divmod(n, 6)
                    if at == 1 and j < 3:
                        w_high("B", l, B_ATT + j + 1, KT)
                    if at == 1 and j == 3:
                        w_high("B", l, B_OUT, KT)
                    if at == 3:
                        w_high("A", l, A_ATT + 2 * j + 2, KT)
                        mixer_centre(j)
                    if at == 5 and j < 3:
                        w_high("A", l, A_ATT + 2 * j + 3, KT)

                act.wait_ge(mixed.sem, mixed.done(l, 3))
                act.wait_ge(o_out.sem, o_out.done(l, N_UNITS - 1))
                act.wait_ge(job_done["A"].sem, job_done["A"].done(l, A_OUT - 1))
                act.wait_ge(job_done["B"].sem, job_done["B"].done(l, B_OUT - 1))
                for t in (4, 5, 6, 7, 0, 1, 2, 3):
                    nc.scalar.activation(in_hi[:, t, :], mix[:, t, :], ACT.Copy,
                                         scale=vc[:, V_MIX + t:V_MIX + t + 1]).then_inc(in_hi_made.sem, 1)
                act.wait_ge(stat_ps.sem, stat_ps.done(l, 1))
                root(r_conv[:], ps["D"][:, 0:T], CONV_W).then_inc(stat_root.sem, 1)
                act.wait_ge(stat_ps.sem, stat_ps.done(l, 2))
                root(r_attn[:], ps["C"][:, 0:T], ATTN_W).then_inc(stat_root.sem, 1)
                with act.Fori(0, 3) as i:
                    w_high("A", l, A_OUT + i + 1, KT)
                    w_high("B", l, B_OUT + i + 1, KT)
                w_high("A", l, A_UP[0], KT)
                w_high("B", l, B_UP[0], KT)
                act.wait_ge(h_done.sem, h_done.done(l, KT - 1))
                for t in range(KT):
                    nc.scalar.activation(in_hi[:, t, :], h[:, t, :], ACT.Copy,
                                         scale=vc[:, V_FFN + t:V_FFN + t + 1]).then_inc(in_hi_made.sem, 1)

                def up_centre_tap(i, n, side):
                    act.wait_ge(emptied["AB"[side]].sem, emptied["AB"[side]].done(l, (A_UP, B_UP)[side][n] + i))
                    act.wait_ge(product.sem, product.done(l, n * HALF + i - 1))
                    if side:
                        act.wait_ge(act_lo_made.sem, act_lo_made.done(l, n * HALF + i - 1))
                    c = V_FCONV + 2 * FF_TILES + side * FF_TILES + n * HALF
                    nc.scalar.activation(up_out[side], up_in[side][:, 1:1 + CW], ACT.Copy,
                                         scale=vc[:, bass.ds(c + i, 1)]).then_inc(up_centre[side].sem, 1)

                def ffn_pair(f, i, kt, k_a, k_b):
                    w_high("A", l, k_a, kt)
                    if isinstance(i, int) and i == 0 and f == 0:
                        act.wait_ge(stat_ps.sem, stat_ps.done(l, 3))
                        root(r_in[:], ps["C"][:, 0:T], D_MODEL).then_inc(stat_root.sem, 1)
                    up_centre_tap(i, f, 0)
                    act.wait_ge(up_right[0].sem, up_right[0].done(l, f * HALF + i))
                    nc.scalar.activation(up_out[0], up_out[0], ACT.Silu).then_inc(silued.sem, 1)
                    w_high("B", l, k_b, kt)
                    up_centre_tap(i, f, 1)
                    act.wait_ge(product.sem, product.done(l, f * HALF + i))
                    if isinstance(i, int) and i == 0:
                        act.wait_ge(job_done["A"].sem, job_done["A"].done(l, A_UP[f] - 1))
                        act.wait_ge(job_done["B"].sem, job_done["B"].done(l, B_UP[f] - 1))
                    nc.scalar.copy(act_hi[:, bass.ds(i, 1), :].rearrange("p a c -> p (a c)"),
                                   up_out[1]).then_inc(act_hi_made.sem, 1)

                for f in range(HALVES):
                    ffn_pair(f, 0, KT, A_UP[f] + 1, B_UP[f] + 1)
                    with act.Fori(1, HALF - 1) as i:
                        ffn_pair(f, i, KT, A_UP[f] + i + 1, B_UP[f] + i + 1)
                    ffn_pair(f, HALF - 1, HALF, A_DOWN[f], B_DOWN[f])
                    with act.Fori(0, 3) as i:
                        w_high("A", l, A_DOWN[f] + i + 1, HALF)
                        w_high("B", l, B_DOWN[f] + i + 1, HALF)
                    w_high("A", l, A_DOWN[f] + 4, KT)
                    w_high("B", l, B_DOWN[f] + 4, KT if f == 0 else KT_PLE)

                act.wait_ge(h_done.sem, h_done.done(l, 3 * KT - 1))
                for t in range(KT):
                    nc.scalar.copy(in_hi[:, t, :], h[:, t, :]).then_inc(in_hi_made.sem, 1)
                act.wait_ge(p_in.sem, p_in.done(l, 0))
                nc.scalar.copy(p_hi[:].rearrange("p k t -> p (k t)"), p_raw).then_inc(p_hi_made.sem, 1)

                def sigmoid(m):
                    act.wait_ge(job_done["A"].sem, job_done["A"].done(l, A_PLE + m))
                    act.wait_ge(gated_p.sem, gated_p.done(l, m - 1))
                    nc.scalar.activation(conv_out[:, 0:T], ps["A"][:, 0:T], ACT.Sigmoid).then_inc(sigmoided.sem, 1)

                with act.Fori(0, 7) as i:
                    w_high("A", l, A_PLE + i + 1, KT)
                    sigmoid(i)
                    w_high("B", l, B_PLE + i + 1, KT_PLE)
                sigmoid(7)

        @block.gpsimd
        def _(pool):
            for e in (*lo_made.values(), squared, z_sq, z_cos, product):
                e.open(pool)
            nc.gpsimd.memset(eps[:], EPS).then_inc(eps_set, 1)

            def w_low(s, l, k, kt):
                pool.wait_ge(hi_made[s].sem, hi_made[s].done(l, k))
                nc.gpsimd.tensor_tensor(w_lo[s][:, 0:kt, :].rearrange("p k n -> p (k n)"), raw[s][:, 0:kt * P],
                                        w_hi[s][:, 0:kt, :].rearrange("p k n -> p (k n)").bitcast(F32),
                                        ALU.subtract).then_inc(lo_made[s].sem, 1)

            def add_square(l, k, src, acc, into):
                pool.wait_ge(summed.sem, summed.done(l, into - 1))
                nc.gpsimd.tensor_tensor(sq[:], src, src, ALU.mult).then_inc(squared.sem, 1)
                pool.wait_ge(squared.sem, squared.done(l, k))
                nc.gpsimd.tensor_tensor(acc[:], acc[:], sq[:], ALU.add).then_inc(summed.sem, 1)

            nc.gpsimd.memset(sum_h[:], 0.0).then_inc(first_sq, 1)
            pool.wait_ge(x_in, 32)
            for t in range(KT):
                pool.wait_ge(first_sq, 2 * t + 1)
                nc.gpsimd.tensor_tensor(sq[:], h[:, t, :], h[:, t, :], ALU.mult).then_inc(first_sq, 1)
                pool.wait_ge(first_sq, 2 * t + 2)
                nc.gpsimd.tensor_tensor(sum_h[:], sum_h[:], sq[:], ALU.add).then_inc(
                    summed.sem if t == KT - 1 else first_sq, 1)

            def z_square(l, r, s, k):
                pool.wait_ge(emptied[s].sem, emptied[s].done(l, k))
                pool.wait_ge(z_scaled.sem, z_scaled.done(l, r - 1))
                nc.gpsimd.tensor_tensor(zsq[:], z[r % 2][:], z[r % 2][:], ALU.mult).then_inc(z_sq.sem, 1)

            def z_cosine(l, r):
                pool.wait_ge(z_scaled.sem, z_scaled.done(l, r))
                pool.wait_ge(z_hi.sem, z_hi.done(l, r - 1))
                pool.wait_ge(z_lo.sem, z_lo.done(l, r - 1))
                nc.gpsimd.tensor_tensor(zcos[:, 0:T], z[r % 2][:], cos_sin[:, 0, :], ALU.mult).then_inc(z_cos.sem, 1)

            pool.wait_ge(const_in, 32)
            with pool.Fori(0, DEPTH) as l:
                w_low("A", l, 0, KT)
                w_low("B", l, 0, KT)
                w_low("A", l, 1, KT)
                z_square(l, 0, "A", 0)
                w_low("B", l, 1, KT)
                z_cosine(l, 0)
                w_low("A", l, 2, KT)
                z_square(l, 1, "A", 1)
                w_low("B", l, 2, KT)
                z_square_next = (("B", 1), ("A", 2), ("B", 2))
                z_cosine(l, 1)
                z_square(l, 2, *z_square_next[0])
                w_low("A", l, A_ATT, KT)
                z_cosine(l, 2)
                z_square(l, 3, *z_square_next[1])
                w_low("B", l, B_ATT, KT)
                z_cosine(l, 3)
                z_square(l, 4, *z_square_next[2])
                z_cosine(l, 4)
                w_low("A", l, A_ATT + 1, KT)

                pool.wait_ge(stat_ps.sem, stat_ps.done(l, 0))
                pool.sem_inc(settled["pool"], 1)
                nc.gpsimd.memset(sum_h[:], 0.0).then_inc(summed.sem, 1)
                nc.gpsimd.memset(sum_c[:], 0.0).then_inc(summed.sem, 1)
                for n in range(N_UNITS):
                    j, at = divmod(n, 6)
                    if at == 1:
                        w_low("B", l, B_ATT + j + 1, KT)
                    if at == 3:
                        w_low("A", l, A_ATT + 2 * j + 2, KT)
                    if at == 5 and j < 3:
                        w_low("A", l, A_ATT + 2 * j + 3, KT)
                    if at == 5:
                        pool.wait_ge(mixed.sem, mixed.done(l, j))
                        add_square(l, 2 * j, mix[:, 4 + j, :], sum_c, 2 + 2 * j)
                        pool.wait_ge(o_out.sem, o_out.done(l, n))
                        add_square(l, 2 * j + 1, mix[:, j, :], sum_h, 3 + 2 * j)

                pool.wait_ge(stat_ps.sem, stat_ps.done(l, 2))
                pool.sem_inc(settled["pool"], 1)
                nc.gpsimd.memset(sum_h[:], 0.0).then_inc(summed.sem, 1)

                def out_squares(m):
                    pool.wait_ge(h_done.sem, h_done.done(l, m))
                    add_square(l, 8 + m, h[:, bass.ds(m, 1), :].rearrange("p a t -> p (a t)"), sum_h, 11 + m)

                with pool.Fori(0, 3) as i:
                    w_low("A", l, A_OUT + i + 1, KT)
                    out_squares(2 * i)
                    w_low("B", l, B_OUT + i + 1, KT)
                    out_squares(2 * i + 1)
                w_low("A", l, A_UP[0], KT)
                out_squares(6)
                w_low("B", l, B_UP[0], KT)
                out_squares(7)

                def multiply(f, i):
                    pool.wait_ge(silued.sem, silued.done(l, f * HALF + i))
                    pool.wait_ge(up_right[1].sem, up_right[1].done(l, f * HALF + i))
                    nc.gpsimd.tensor_tensor(up_out[1], up_out[0], up_out[1], ALU.mult).then_inc(product.sem, 1)

                for f in range(HALVES):
                    with pool.Fori(0, HALF - 1) as i:
                        w_low("A", l, A_UP[f] + i + 1, KT)
                        w_low("B", l, B_UP[f] + i + 1, KT)
                        multiply(f, i)
                    w_low("A", l, A_DOWN[f], HALF)
                    w_low("B", l, B_DOWN[f], HALF)
                    multiply(f, HALF - 1)
                    with pool.Fori(0, 3) as i:
                        w_low("A", l, A_DOWN[f] + i + 1, HALF)
                        w_low("B", l, B_DOWN[f] + i + 1, HALF)
                    w_low("A", l, A_DOWN[f] + 4, KT)
                    w_low("B", l, B_DOWN[f] + 4, KT if f == 0 else KT_PLE)

                pool.wait_ge(stat_ps.sem, stat_ps.done(l, 3))
                pool.sem_inc(settled["pool"], 1)
                nc.gpsimd.memset(sum_h[:], 0.0).then_inc(summed.sem, 1)

                def ple_squares(m):
                    pool.wait_ge(h_done.sem, h_done.done(l, 3 * KT + m))
                    add_square(l, 16 + m, h[:, bass.ds(m, 1), :].rearrange("p a t -> p (a t)"), sum_h, 20 + m)

                w_low("A", l, A_PLE + 1, KT)
                w_low("B", l, B_PLE + 1, KT_PLE)
                with pool.Fori(0, 6) as i:
                    w_low("A", l, A_PLE + i + 2, KT)
                    ple_squares(i)
                    w_low("B", l, B_PLE + i + 2, KT_PLE)
                ple_squares(6)
                ple_squares(7)

        @block.vector
        def _(dve):
            for e in (*emptied.values(), in_lo_made, stat_ready, z_inv, z_scaled, z_sin, z_roped, z_lo,
                      v_lo, padded, gated, left, right, mixed, topped, neg_topped, inverted, normed, pt_lo_made,
                      o_out, *scaled.values(), added, *up_left, *up_right, act_lo_made, p_lo_made, gated_p):
                e.open(dve)
            dve.wait_ge(x_in, 32)
            h_done.open(dve)
            dve.wait_ge(const_in, 32)

            def low(l, phase, n, t, src, gain):
                dve.wait_ge(in_hi_made.sem, in_hi_made.done(l, phase * KT + n))
                hi = in_hi[:, t, :].bitcast(F32)
                if gain is None:
                    ins = nc.vector.tensor_tensor(in_lo[:, t, :], src, hi, ALU.subtract)
                else:
                    ins = nc.vector.scalar_tensor_tensor(in_lo[:, t, :], src, vc[:, gain:gain + 1], hi,
                                                         ALU.mult, ALU.subtract)
                ins.then_inc(in_lo_made.sem, 1)

            def recip(l, n, r):
                dve.wait_ge(stat_root.sem, stat_root.done(l, n))
                nc.vector.reciprocal(r[:], r[:]).then_inc(stat_ready.sem, 1)

            def pads(l, k, bufs):
                ins = None
                for b in bufs:
                    for c in PADS:
                        ins = nc.vector.memset(b[:, c], 0.0)
                ins.then_inc(padded.sem, 1)

            def empty(s, l, k, out):
                dve.wait_ge(job_done[s].sem, job_done[s].done(l, k))
                if out.shape[-1] == UW:
                    nc.vector.tensor_tensor(out[:, U_PROMPT], ps[s][:, 0:SEQ], r_in[:, 0:SEQ], ALU.mult)
                    ins = nc.vector.tensor_tensor(out[:, U_SAMPLE], ps[s][:, SEQ:T], r_in[:, SEQ:T], ALU.mult)
                else:
                    ins = nc.vector.tensor_tensor(out, ps[s][:, 0:T], r_in[:], ALU.mult)
                ins.then_inc(emptied[s].sem, 1)

            def z_scale(l, r):
                dve.wait_ge(z_root.sem, z_root.done(l, r))
                nc.vector.reciprocal(zsq[:], zsq[:]).then_inc(z_inv.sem, 1)
                dve.wait_ge(z_inv.sem, z_inv.done(l, r))
                gain = V_QG if r else V_KG
                nc.vector.scalar_tensor_tensor(z[r % 2][:], z[r % 2][:], vc[:, gain:gain + 1], zsq[:],
                                               ALU.mult, ALU.mult).then_inc(z_scaled.sem, 1)

            def z_rope(l, r):
                dve.wait_ge(z_swapped.sem, z_swapped.done(l, 4 * r + 3))
                nc.vector.tensor_tensor(zrot[:], zrot[:], cos_sin[:, 1, :], ALU.mult).then_inc(z_sin.sem, 1)
                dve.wait_ge(z_sin.sem, z_sin.done(l, r))
                dve.wait_ge(z_cos.sem, z_cos.done(l, r))
                nc.vector.tensor_tensor(zcos[:, 0:T], zcos[:, 0:T], zrot[:], ALU.add).then_inc(z_roped.sem, 1)
                dve.wait_ge(z_hi.sem, z_hi.done(l, r))
                nc.vector.tensor_tensor(qk_lo[:], zcos[:, 0:T], qk_hi[:].bitcast(F32), ALU.subtract).then_inc(z_lo.sem, 1)

            with dve.Fori(0, DEPTH) as l:
                dve.wait_ge(vec_set.sem, vec_set.done(l, 0))
                for t in range(KT):
                    low(l, 0, t, t, h[:, t, :], V_ATTN + t)
                recip(l, 0, r_in)
                dve.wait_ge(stat_ready.sem, stat_ready.done(l, 0))
                empty("A", l, 0, z[0][:])
                z_scale(l, 0)
                empty("B", l, 0, z[1][:])
                z_rope(l, 0)
                dve.wait_ge(v_turned.sem, v_turned.done(l, 0))
                dve.wait_ge(v_hi.sem, v_hi.done(l, 0))
                nc.vector.tensor_tensor(v_hl[:, :, :, 64:128],
                                        ps["D"][:, 0:T].rearrange("p (t g d) -> p t g d", g=N_KV, d=HEAD_DIM),
                                        v_hl[:, :, :, 0:64].bitcast(F32), ALU.subtract).then_inc(v_lo.sem, 1)
                empty("A", l, 1, z[1][:])
                z_scale(l, 1)
                dve.wait_ge(z_cos.sem, z_cos.done(l, 0))
                dve.wait_ge(z_swapped.sem, z_swapped.done(l, 3))
                empty("B", l, 1, z[0][:])
                z_rope(l, 1)
                z_scale(l, 2)
                empty("A", l, 2, z[1][:])
                z_rope(l, 2)
                z_scale(l, 3)
                empty("B", l, 2, z[0][:])
                z_rope(l, 3)
                z_scale(l, 4)
                z_rope(l, 4)
                pads(l, 0, [conv_in])
                dve.wait_ge(padded.sem, padded.done(l, 0))

                def top_of(n, t):
                    nk, c = unit_of(n)[3], 2 * (n % 2) + t
                    dve.wait_ge(scored.sem, scored.done(l, 2 * n + t))
                    nc.vector.reduce_max(top[:, c:c + 1], ps["C"][:, t * 512:t * 512 + nk], AX_X).then_inc(topped.sem, 1)
                    dve.wait_ge(topped.sem, topped.done(l, 2 * n + t))
                    nc.vector.tensor_scalar(neg_top[:, c:c + 1], top[:, c:c + 1], -SCALE, None,
                                            ALU.mult).then_inc(neg_topped.sem, 1)

                def norm(n, t):
                    nk, c = unit_of(n)[3], 2 * (n % 2) + t
                    dve.wait_ge(exped.sem, exped.done(l, 2 * n + t))
                    nc.vector.reciprocal(inv_total[:, c:c + 1], total[:, c:c + 1]).then_inc(inverted.sem, 1)
                    dve.wait_ge(inverted.sem, inverted.done(l, 2 * n + t))
                    a = probs[:, n % 2, t, 0:nk]
                    nc.vector.tensor_scalar(a, a, inv_total[:, c:c + 1], None, ALU.mult).then_inc(normed.sem, 1)

                def pt_low(n, t):
                    nb = unit_of(n)[3] // P
                    dve.wait_ge(pt_hi_made.sem, pt_hi_made.done(l, 2 * n + t))
                    nc.vector.tensor_tensor(pt_lo[:, 0:nb, t * P:(t + 1) * P],
                                            ps["D"][:, 0:nb * P].rearrange("p (b q) -> p b q", q=P),
                                            pt_hi[:, 0:nb, t * P:(t + 1) * P].bitcast(F32),
                                            ALU.subtract).then_inc(pt_lo_made.sem, 1)

                def mixer(j):
                    empty("A", l, A_ATT + 2 * j + 1, conv_out[:, 0:T])
                    dve.wait_ge(emptied["A"].sem, emptied["A"].done(l, A_ATT + 2 * j + 1))
                    nc.vector.tensor_tensor(conv_in[:, U_PROMPT], conv_in[:, U_PROMPT], conv_out[:, 0:SEQ], ALU.mult)
                    nc.vector.tensor_tensor(conv_in[:, U_SAMPLE], conv_in[:, U_SAMPLE], conv_out[:, SEQ:T],
                                            ALU.mult).then_inc(gated.sem, 1)

                def mixer_taps(j):
                    dve.wait_ge(centre.sem, centre.done(l, j))
                    c = V_MCONV + j
                    nc.vector.scalar_tensor_tensor(conv_out[:], conv_in[:, 0:CW], vc[:, c:c + 1], conv_out[:],
                                                   ALU.mult, ALU.add).then_inc(left.sem, 1)
                    dve.wait_ge(left.sem, left.done(l, j))
                    nc.vector.scalar_tensor_tensor(conv_out[:], conv_in[:, 2:2 + CW], vc[:, c + 8:c + 9], conv_out[:],
                                                   ALU.mult, ALU.add).then_inc(right.sem, 1)
                    dve.wait_ge(right.sem, right.done(l, j))
                    gb = mix[:, 4 + j, :]
                    nc.vector.tensor_tensor(gb[:, 0:SEQ], gb[:, 0:SEQ], conv_out[:, C_PROMPT], ALU.mult)
                    nc.vector.tensor_tensor(gb[:, SEQ:T], gb[:, SEQ:T], conv_out[:, C_SAMPLE],
                                            ALU.mult).then_inc(mixed.sem, 1)

                empty("A", l, A_ATT, mix[:, 4, :])
                top_of(0, 0)
                top_of(0, 1)
                norm(0, 0)
                norm(0, 1)
                for n in range(N_UNITS):
                    j, at = divmod(n, 6)
                    if n + 1 < N_UNITS:
                        top_of(n + 1, 0)
                        top_of(n + 1, 1)
                    pt_low(n, 0)
                    if n + 1 < N_UNITS:
                        norm(n + 1, 0)
                    pt_low(n, 1)
                    if n + 1 < N_UNITS:
                        norm(n + 1, 1)
                    head, q0 = unit_of(n)[:2]
                    dve.wait_ge(o_low_out.sem, o_low_out.done(l, n))
                    r = 64 * (head % 2)
                    nc.vector.tensor_tensor(mix[r:r + 64, j, q0:q0 + UQ], ps["D"][0:64, 512:512 + UQ], o_low[:],
                                            ALU.add).then_inc(o_out.sem, 1)
                    if at == 1:
                        empty("B", l, B_ATT + j, conv_in)
                        dve.wait_ge(emptied["B"].sem, emptied["B"].done(l, B_ATT + j))
                    if at == 3:
                        mixer(j)
                    if at == 4:
                        mixer_taps(j)
                    if at == 5 and j < 3:
                        empty("A", l, A_ATT + 2 * j + 2, mix[:, 5 + j, :])

                for n, t in enumerate((4, 5, 6, 7, 0, 1, 2, 3)):
                    low(l, 1, n, t, mix[:, t, :], V_MIX + t)
                recip(l, 1, r_conv)
                recip(l, 2, r_attn)
                dve.wait_ge(stat_ready.sem, stat_ready.done(l, 2))
                dve.sem_inc(settled["dve"], 1)
                t_conv, t_attn = conv_in[:, 0:T], conv_out[:, 0:T]

                def out_tile(s, k, m):
                    attn_ps, conv_ps = ("A", "B") if s == "A" else ("C", "D")
                    dve.wait_ge(job_done[s].sem, job_done[s].done(l, k))
                    dve.wait_ge(h_done.sem, h_done.done(l, m - 1))
                    nc.vector.tensor_tensor(t_conv, ps[conv_ps][:, 0:T], r_conv[:], ALU.mult).then_inc(
                        scaled["conv"].sem, 1)
                    nc.vector.tensor_tensor(t_attn, ps[attn_ps][:, 0:T], r_attn[:], ALU.mult).then_inc(
                        emptied[s].sem, 1)
                    dve.wait_ge(scaled["conv"].sem, scaled["conv"].done(l, m))
                    dst = h[:, bass.ds(m, 1), :].rearrange("p a t -> p (a t)")
                    nc.vector.tensor_tensor(dst, dst, t_conv, ALU.add).then_inc(added.sem, 1)
                    dve.wait_ge(added.sem, added.done(l, m))
                    dve.wait_ge(emptied[s].sem, emptied[s].done(l, k))
                    nc.vector.tensor_tensor(dst, dst, t_attn, ALU.add).then_inc(h_done.sem, 1)

                with dve.Fori(0, 4) as i:
                    out_tile("A", A_OUT + i, 2 * i)
                    out_tile("B", B_OUT + i, 2 * i + 1)
                for t in range(KT):
                    low(l, 2, t, t, h[:, t, :], V_FFN + t)

                pads(l, 1, up_in)
                recip(l, 3, r_in)
                dve.wait_ge(stat_ready.sem, stat_ready.done(l, 3))

                def up_taps(f, i, side):
                    n = f * HALF + i
                    dve.wait_ge(up_centre[side].sem, up_centre[side].done(l, n))
                    c = V_FCONV + side * FF_TILES + f * HALF
                    out = up_out[side]
                    nc.vector.scalar_tensor_tensor(out, up_in[side][:, 0:CW], vc[:, bass.ds(c + i, 1)], out,
                                                   ALU.mult, ALU.add).then_inc(up_left[side].sem, 1)
                    dve.wait_ge(up_left[side].sem, up_left[side].done(l, n))
                    nc.vector.scalar_tensor_tensor(out, up_in[side][:, 2:2 + CW],
                                                   vc[:, bass.ds(c + 4 * FF_TILES + i, 1)], out,
                                                   ALU.mult, ALU.add).then_inc(up_right[side].sem, 1)

                def ffn_pair(f, i):
                    dve.wait_ge(up_right[0].sem, up_right[0].done(l, f * HALF + i - 1))
                    empty("A", l, A_UP[f] + i, up_in[0])
                    up_taps(f, i, 0)
                    dve.wait_ge(up_right[1].sem, up_right[1].done(l, f * HALF + i - 1))
                    empty("B", l, B_UP[f] + i, up_in[1])
                    up_taps(f, i, 1)
                    dve.wait_ge(act_hi_made.sem, act_hi_made.done(l, f * HALF + i))
                    dst = act_lo[:, bass.ds(i, 1), :].rearrange("p a c -> p (a c)")
                    hi = act_hi[:, bass.ds(i, 1), :].rearrange("p a c -> p (a c)").bitcast(F32)
                    nc.vector.tensor_tensor(dst, up_out[1], hi, ALU.subtract).then_inc(act_lo_made.sem, 1)

                def down_tile(s, k, f, m):
                    dve.wait_ge(job_done[s].sem, job_done[s].done(l, k))
                    dst = h[:, bass.ds(m, 1), :].rearrange("p a t -> p (a t)")
                    nc.vector.tensor_tensor(dst, ps[s][:, 0:T], dst, ALU.add).then_inc(h_done.sem, 1)
                    dve.wait_ge(h_done.sem, h_done.done(l, (1 + f) * KT + m))
                    emptied[s].open(dve)

                dve.wait_ge(padded.sem, padded.done(l, 1))
                dve.sem_inc(settled["dve"], 1)
                for f in range(HALVES):
                    with dve.Fori(0, HALF) as i:
                        ffn_pair(f, i)
                    with dve.Fori(0, 4) as i:
                        down_tile("A", A_DOWN[f] + i, f, 2 * i)
                        down_tile("B", B_DOWN[f] + i, f, 2 * i + 1)

                for t in range(KT):
                    low(l, 3, t, t, h[:, t, :], None)
                dve.wait_ge(p_hi_made.sem, p_hi_made.done(l, 0))
                nc.vector.tensor_tensor(p_lo[:].rearrange("p k t -> p (k t)"), p_raw,
                                        p_hi[:].rearrange("p k t -> p (k t)").bitcast(F32),
                                        ALU.subtract).then_inc(p_lo_made.sem, 1)
                with dve.Fori(0, 8) as m:
                    dve.wait_ge(sigmoided.sem, sigmoided.done(l, m))
                    emptied["A"].open(dve)
                    dve.wait_ge(job_done["B"].sem, job_done["B"].done(l, B_PLE + m))
                    dve.wait_ge(h_done.sem, h_done.done(l, 3 * KT + m - 1))
                    nc.vector.tensor_tensor(conv_in[:, 0:T], ps["B"][:, 0:T], conv_out[:, 0:T],
                                            ALU.mult).then_inc(gated_p.sem, 1)
                    dve.wait_ge(gated_p.sem, gated_p.done(l, m))
                    emptied["B"].open(dve)
                    dst = h[:, bass.ds(m, 1), :].rearrange("p a t -> p (a t)")
                    nc.vector.tensor_tensor(dst, dst, conv_in[:, 0:T], ALU.add).then_inc(h_done.sem, 1)


def _weight_tiles(w, kt):
    depth, _, cols = w.shape
    a = w.reshape(depth, kt, P, cols // P, P).transpose(0, 3, 2, 1, 4)
    return a.reshape(depth * (cols // P), P, kt * P)


def _rope_tables():
    half = HEAD_DIM // 2
    freqs = np.float32(ROPE_THETA) ** (-np.arange(0, half, 2, dtype=np.float32) / np.float32(half))
    pos = np.arange(SEQ)
    row, col = (pos // GRID_W).astype(np.float32), (pos % GRID_W).astype(np.float32)
    ang = np.concatenate([row[:, None] * freqs, row[:, None] * freqs,
                          col[:, None] * freqs, col[:, None] * freqs], axis=1)
    sign = np.repeat(np.array([-1, 1, -1, 1], np.float32), HEAD_DIM // 4)
    cos, sin = np.cos(ang).T[ROPE_ORDER], (np.sin(ang) * sign).T[ROPE_ORDER]
    both = [np.tile(np.concatenate([t, t[:, :DEC_SEQ]], axis=1), (2, 1)) for t in (cos, sin)]
    return np.ascontiguousarray(np.stack(both, axis=1), dtype=np.float32)


def kernel(**inputs):
    import concourse.bacc as bacc
    from concourse.bass_utils import run_bass_kernel_spmd

    a = {k: np.asarray(v) for k, v in inputs.items()}

    def channels(prompt, sample, n):
        both = np.concatenate([prompt, sample], axis=0).T
        return both.reshape(n, P, T).transpose(1, 0, 2)

    def columns(v):
        return v.reshape(-1, P).T

    vec = []
    for l in range(DEPTH):
        vec.append(np.concatenate([columns(a["attn_norm_g"][l]), columns(a["ffn_norm_g"][l]), columns(a["attn_out_g"][l]),
                columns(a["conv_out_g"][l]), np.tile(a["q_norm_g"][l][ROPE_ORDER], 2)[:, None],
                np.tile(a["k_norm_g"][l][ROPE_ORDER], 2)[:, None], columns(a["mix_conv_w"][l]), columns(a["ffn_conv_w"][l])], axis=1))
    qk_w = ATTN_W + N_KV * HEAD_DIM
    in_order = [HEAD_DIM * head + c for head in range(qk_w // HEAD_DIM) for c in ROPE_ORDER]
    in_order += range(qk_w, D_IN)
    eye = np.eye(P, dtype=np.float32)
    heads = np.kron(np.eye(2, dtype=np.float32), np.ones((HEAD_DIM, HEAD_DIM), np.float32))
    w_down = a["w_down"].reshape(DEPTH * HALVES, HALF * P, D_MODEL)
    arrays = {
        "x": channels(a["x_prompt"][0], a["x_sample"][0], KT),
        "p": np.stack([channels(a["p_prompt"][l, 0], a["p_sample"][l, 0], KT_PLE).reshape(P, KT_PLE * T)
                       for l in range(DEPTH)]),
        "w_in": _weight_tiles(a["w_in"][:, :, in_order], KT), "w_out": _weight_tiles(a["w_out"], KT),
        "w_up": _weight_tiles(a["w_up"], KT), "w_down": _weight_tiles(w_down, HALF),
        "w_gate": _weight_tiles(a["w_ple_gate"], KT), "w_proj": _weight_tiles(a["w_ple_proj"], KT_PLE),
        "vec": np.stack(vec), "tables": _rope_tables(),
        "mats": np.stack([eye, np.ones((P, P), np.float32), heads], axis=1),
    }
    nc = bacc.Bacc("TRN2", target_bir_lowering=False, num_devices=1, dynamic_dma_scratch_size=1024)
    arrays = {f"in_{k}": np.ascontiguousarray(v) for k, v in arrays.items()}
    args = [nc.dram_tensor(k, v.shape, F32, kind="ExternalInput").ap() for k, v in arrays.items()]
    y = nc.dram_tensor("out_y", (P, KT, T), F32, kind="ExternalOutput").ap()
    trunk_program(nc, *args, y)
    r = run_bass_kernel_spmd(nc, [arrays], core_ids=[0])
    out = r.results[0]["out_y"].transpose(1, 0, 2).reshape(D_MODEL, T).T
    return (np.ascontiguousarray(out[:SEQ])[None], np.ascontiguousarray(out[SEQ:])[None])
```

```python
from contextlib import ExitStack

import numpy as np

import concourse.bass as bass
from concourse import mybir

F32 = mybir.dt.float32
F32R = mybir.dt.float32r
ALU = mybir.AluOpType
ACT = mybir.ActivationFunctionType
AX_X = mybir.AxisListType.X

P = 128
DEPTH, D_MODEL, SEQ, DEC_SEQ = 2, 1024, 512, 256
T = SEQ + DEC_SEQ
HEAD_DIM, N_HEADS, N_KV = 64, 8, 2
Q_PER_KV = N_HEADS // N_KV
ATTN_W, CONV_W, D_FF, PLE_DIM = 512, 512, 2816, 256
D_IN = ATTN_W + 2 * N_KV * HEAD_DIM + 3 * CONV_W
GRID_W, ROPE_THETA, EPS = 64, 10000.0, 1e-6
SCALE = HEAD_DIM ** -0.5

KT = D_MODEL // P
IN_TILES = D_IN // P
FF_TILES = D_FF // P
HALVES = 2
HALF = FF_TILES // HALVES
KT_PLE = PLE_DIM // P
CHUNKS = ((0, SEQ), (SEQ, T))

UW = T + 4
CW = T + 2
U_PROMPT, U_SAMPLE = slice(1, 1 + SEQ), slice(SEQ + 3, SEQ + 3 + DEC_SEQ)
C_PROMPT, C_SAMPLE = slice(0, SEQ), slice(SEQ + 2, CW)
PADS = (slice(0, 1), slice(SEQ + 1, SEQ + 3), slice(UW - 1, UW))

IN_ORDER = [4, 0, 1, 2, 3, 5] + [t + j for j in range(4) for t in (6, 10, 14)]
N_QKV, N_MIX = 6, 12

ROPE_ORDER = [16 * b + i for b in (0, 2, 1, 3) for i in range(16)]

AT_QKV, AT_MIX = 0, N_QKV // 2
AT_OUT = AT_MIX + N_MIX // 2
AT_UP = [AT_OUT + 4, AT_OUT + 4 + HALF + 4]
AT_DOWN = [a + HALF for a in AT_UP]
AT_PLE = AT_DOWN[1] + 4
N_USES = AT_PLE + 4

V_ATTN, V_FFN, V_MIX, V_QG, V_KG, V_MCONV = 0, 8, 16, 24, 25, 26
V_FCONV = V_MCONV + 3 * 4
N_VEC = V_FCONV + 3 * 2 * FF_TILES

UNITS = ((0, 0, SEQ), (256, 0, SEQ), (SEQ, SEQ, DEC_SEQ))
UQ = 256
N_UNITS = N_HEADS * len(UNITS)

MIX_ORDER = (0, 1, 2, 4, 5, 6, 3, 7)
PIECES = [3 if n % 3 == 2 else 4 for n in range(N_UNITS)]
ENDS = [[q for q in range(1, N_MIX) if sum(PIECES[:n]) < KT * q <= sum(PIECES[:n + 1])] for n in range(N_UNITS)]
assert sum(PIECES) == KT * (N_MIX - 1)


def slot_of(g):
    return "AB"[g % 2], g // 2


def mix_job(q):
    return slot_of(N_QKV + q)


class Event:

    def __init__(self, sem, per_layer, by=1):
        self.sem, self.per_layer, self.by = sem, per_layer, by

    def done(self, layer, k):
        return (layer * self.per_layer + k + 2) * self.by

    def open(self, eng):
        eng.sem_inc(self.sem, self.by)


def trunk_program(nc, x, p, w_in, w_out, w_up, w_down, w_gate, w_proj, vec, tables, mats, y):
    with ExitStack() as ctx:
        def sb(name, shape, dt=F32, where=ctx):
            return where.enter_context(nc.sbuf_tensor(name, shape, dt))

        def event(name, per_layer, by=1):
            return Event(ctx.enter_context(nc.semaphore(name)), per_layer, by)

        h = sb("h", [P, KT, T])
        in_hi, in_lo = sb("in_hi", [P, KT, T], F32R), sb("in_lo", [P, KT, T], F32R)
        raw = {s: sb(f"raw{s}", [P, HALF * P]) for s in "AB"}
        w_hi = {s: sb(f"w_hi{s}", [P, HALF, P], F32R) for s in "AB"}
        w_lo = {s: sb(f"w_lo{s}", [P, HALF, P], F32R) for s in "AB"}
        mix = sb("mix", [P, KT, T])
        mix_flat = mix[:].rearrange("p k t -> p (k t)")
        conv_in, conv_out = sb("conv_in", [P, UW]), sb("conv_out", [P, CW])
        cos_sin = sb("cos_sin", [P, 2, T])
        r_in, r_attn, r_conv = sb("r_in", [P, T]), sb("r_attn", [P, T]), sb("r_conv", [P, T])
        sum_h = sb("sum_h", [P, T])
        mat = sb("mat", [P, 3, P])
        ident, ones, head_ones = mat[:, 0, :], mat[:, 1, :], mat[:, 2, :]
        vc = sb("vc", [P, N_VEC])
        eps = sb("eps", [P, 1])
        top, neg_top, total, inv_total = (sb(n, [P, 4]) for n in ("top", "neg_top", "total", "inv_total"))
        with ExitStack() as att:
            q_st = sb("q_st", [P, N_HEADS, T], F32R, att)
            k_hi, k_lo = sb("k_hi", [P, N_KV, T], F32R, att), sb("k_lo", [P, N_KV, T], F32R, att)
            v_hl = sb("v_hl", [P, T // P, N_KV, 2 * HEAD_DIM], F32R, att)
            with ExitStack() as units:
                pt_hi = sb("pt_hi", [P, SEQ // P, UQ], F32R, units)
                pt_lo = sb("pt_lo", [P, SEQ // P, UQ], F32R, units)
                probs = sb("probs", [P, 2, 2, SEQ], F32, units)
                o_low = sb("o_low", [HEAD_DIM, UQ], F32, units)
            z = [sb(f"z{i}", [P, T], F32, att) for i in range(2)]
            zsq, zrot = sb("zsq", [P, T], F32, att), sb("zrot", [P, T], F32, att)
            qk_hi, qk_lo = sb("qk_hi", [P, T], F32R, att), sb("qk_lo", [P, T], F32R, att)
            sum_c, sq = sb("sum_c", [P, T], F32, att), sb("sq", [P, T], F32, att)
        with ExitStack() as out:
            mix_hi, mix_lo = sb("mix_hi", [P, KT, T], F32R, out), sb("mix_lo", [P, KT, T], F32R, out)
        with ExitStack() as ple:
            p_hi, p_lo = sb("p_hi", [P, KT_PLE * T], F32R, ple), sb("p_lo", [P, KT_PLE * T], F32R, ple)
            proj_hi = sb("proj_hi", [P, 8 * KT_PLE * P], F32R, ple)
            proj_lo = sb("proj_lo", [P, 8 * KT_PLE * P], F32R, ple)
            gate = [sb(f"gate{i}", [P, T], F32, ple) for i in range(2)]
            gated_p = [sb(f"gated_p{i}", [P, T], F32, ple) for i in range(2)]
        act_hi, act_lo = sb("act_hi", [P, HALF, CW], F32R), sb("act_lo", [P, HALF, CW], F32R)
        zcos = conv_out
        up_in = [mix_flat[:, i * UW:(i + 1) * UW] for i in range(2)]
        up_out = [mix_flat[:, 2 * UW + i * CW:2 * UW + (i + 1) * CW] for i in range(2)]
        p_raw = mix_flat[:, 2 * UW + 2 * CW:2 * UW + 2 * CW + KT_PLE * T]
        proj_raw = mix_flat[:, 0:8 * KT_PLE * P]

        ps = {n: ctx.enter_context(nc.psum_tensor(f"ps{n}", [P, 1024], F32)) for n in "ABCD"}

        raw_in = {s: event(f"raw_in_{s}", N_USES, 16) for s in "AB"}
        hi_made = {s: event(f"hi_made_{s}", N_USES) for s in "AB"}
        lo_made = {s: event(f"lo_made_{s}", N_USES) for s in "AB"}
        job_done = {s: event(f"job_done_{s}", N_USES) for s in "AB"}
        emptied = {s: event(f"emptied_{s}", N_USES) for s in "AB"}
        vec_set = event("vec_set", 1, 16)
        in_hi_made, in_lo_made = event("in_hi_made", 3 * KT), event("in_lo_made", 3 * KT)
        mix_hi_made, mix_lo_made = event("mix_hi_made", KT), event("mix_lo_made", KT)
        h_done = event("h_done", 4 * KT)
        squared, summed = event("squared", 24), event("summed", 28)
        stat_ps, stat_root, stat_ready = event("stat_ps", 4), event("stat_root", 4), event("stat_ready", 4)
        z_sq, z_ss, z_root = event("z_sq", 5), event("z_ss", 5), event("z_root", 5)
        z_inv, z_scaled = event("z_inv", 5), event("z_scaled", 5)
        z_swapped = event("z_swapped", 20, 16)
        z_cos, z_sin, z_roped = event("z_cos", 5), event("z_sin", 5), event("z_roped", 5)
        z_hi, z_lo = event("z_hi", 5), event("z_lo", 5)
        qk_placed = event("qk_placed", 8 + 4 * 4, 16)
        v_turned, v_hi, v_lo = event("v_turned", 1), event("v_hi", 1), event("v_lo", 1)
        padded = event("padded", 2)
        gated, centre, left, right, mixed = (event(n, 4) for n in ("gated", "centre", "left", "right", "mixed"))
        nq = 2 * N_UNITS
        scored, topped, neg_topped, exped = (event(n, nq) for n in ("scored", "topped", "neg_topped", "exped"))
        inverted, normed, turned, pt_hi_made, pt_lo_made = (
            event(n, nq) for n in ("inverted", "normed", "turned", "pt_hi_made", "pt_lo_made"))
        weighed, o_low_out, o_out = (event(n, N_UNITS) for n in ("weighed", "o_low_out", "o_out"))
        scaled = {"conv": event("scaled_conv", 8), "attn": event("scaled_attn", 8)}
        added = event("added", 8)
        up_centre = [event(f"up_centre{i}", FF_TILES) for i in range(2)]
        up_left = [event(f"up_left{i}", FF_TILES) for i in range(2)]
        up_right = [event(f"up_right{i}", FF_TILES) for i in range(2)]
        silued, product = event("silued", FF_TILES), event("product", FF_TILES)
        act_hi_made, act_lo_made = event("act_hi_made", FF_TILES), event("act_lo_made", FF_TILES)
        p_in, p_hi_made, p_lo_made = event("p_in", 1, 16), event("p_hi_made", 1), event("p_lo_made", 1)
        proj_in, proj_hi_made, proj_lo_made = event("proj_in", 1, 16), event("proj_hi_made", 1), event("proj_lo_made", 1)
        sigmoided, proj_done, p_gated = event("sigmoided", 8), event("proj_done", 8), event("p_gated", 8)
        const_in = ctx.enter_context(nc.semaphore("const_in"))
        x_in = [ctx.enter_context(nc.semaphore(f"x_in{t}")) for t in range(KT)]
        tables_in = ctx.enter_context(nc.semaphore("tables_in"))
        eps_set = ctx.enter_context(nc.semaphore("eps_set"))
        x_sq, x_sum = (ctx.enter_context(nc.semaphore(n)) for n in ("x_sq", "x_sum"))
        y_out = ctx.enter_context(nc.semaphore("y_out"))

        settled = {e: ctx.enter_context(nc.semaphore(f"settled_{e}")) for e in ("pool", "dve", "sp")}

        def unit_of(n):
            return (n // 3,) + UNITS[n % 3]

        block = ctx.enter_context(nc.Block())

        @block.sync
        def _(sp):
            for e in (*raw_in.values(), vec_set, z_swapped, qk_placed, p_in, proj_in):
                e.open(sp)
            sp.dma_start(mat[:], mats).then_inc(const_in, 16)
            for t in range(KT):
                sp.dma_start(h[:, t, :], x[:, t, :]).then_inc(x_in[t], 16)

            def load(s, l, k, src, kt):
                w, tile = src
                at = sp.snap(tile)
                sp.wait_ge(lo_made[s].sem, lo_made[s].done(l, k - 1))
                sp.dma_start(raw[s][:, 0:kt * P], w[at]).then_inc(raw_in[s].sem, 16)

            def swap(l, r):
                sp.wait_ge(z_scaled.sem, z_scaled.done(l, r))
                sp.sem_inc(settled["sp"], 1)
                sp.wait_ge(z_roped.sem, z_roped.done(l, r - 1))
                for to, of in ((0, 32), (32, 0), (64, 96), (96, 64)):
                    sp.dma_start(zrot[to:to + 32, :], z[r % 2][of:of + 32, :]).then_inc(z_swapped.sem, 16)

            def place_k(l):
                sp.wait_ge(z_lo.sem, z_lo.done(l, 0))
                for g in range(N_KV):
                    for half in range(2):
                        rows = slice(half * 64, half * 64 + 64)
                        for dst, src in ((k_hi, qk_hi), (k_lo, qk_lo)):
                            sp.dma_start(dst[rows, g, :].bitcast(F32), src[g * 64:g * 64 + 64, :].bitcast(F32)).then_inc(qk_placed.sem, 16)

            def place_q(l, j):
                sp.wait_ge(z_lo.sem, z_lo.done(l, j + 1))
                for hh in range(2):
                    for half, src in enumerate((qk_hi, qk_lo)):
                        sp.dma_start(q_st[half * 64:half * 64 + 64, 2 * j + hh, :].bitcast(F32),
                                     src[hh * 64:hh * 64 + 64, :].bitcast(F32)).then_inc(qk_placed.sem, 16)

            with sp.Fori(0, DEPTH) as l:
                def w_in_load(g):
                    s, k = slot_of(g)
                    load(s, l, k, (w_in, l * IN_TILES + IN_ORDER[g]), KT)

                layer = sp.snap(l)
                sp.wait_ge(act_lo_made.sem, act_lo_made.done(l, -1))
                sp.dma_start(vc[:], vec[layer]).then_inc(vec_set.sem, 16)
                for g in range(4):
                    w_in_load(g)
                for r in range(5):
                    w_in_load(4 + r)
                    swap(l, r)
                    if r == 0:
                        place_k(l)
                    else:
                        place_q(l, r - 1)
                for g in range(9, N_QKV + N_MIX):
                    w_in_load(g)
                with sp.Fori(0, 4) as i:
                    load("A", l, AT_OUT + i, (w_out, l * 8 + 2 * i), KT)
                    load("B", l, AT_OUT + i, (w_out, l * 8 + 2 * i + 1), KT)
                layer = sp.snap(l)
                sp.wait_ge(mix_lo_made.sem, mix_lo_made.done(l, KT - 1))
                sp.dma_start(p_raw, p[layer]).then_inc(p_in.sem, 16)
                for f in range(HALVES):
                    with sp.Fori(0, HALF) as i:
                        load("A", l, AT_UP[f] + i, (w_up, l * 2 * FF_TILES + f * HALF + i), KT)
                        load("B", l, AT_UP[f] + i, (w_up, l * 2 * FF_TILES + FF_TILES + f * HALF + i), KT)
                    with sp.Fori(0, 4) as i:
                        load("A", l, AT_DOWN[f] + i, (w_down, (l * HALVES + f) * 8 + 2 * i), HALF)
                        load("B", l, AT_DOWN[f] + i, (w_down, (l * HALVES + f) * 8 + 2 * i + 1), HALF)
                    if f == 1:
                        layer = sp.snap(l)
                        sp.wait_ge(act_lo_made.sem, act_lo_made.done(l, FF_TILES - 1))
                        sp.dma_start(proj_raw, w_proj[layer]).then_inc(proj_in.sem, 16)
                with sp.Fori(0, 4) as i:
                    load("A", l, AT_PLE + i, (w_gate, l * 8 + 2 * i), KT)
                    load("B", l, AT_PLE + i, (w_gate, l * 8 + 2 * i + 1), KT)
            for m in range(KT):
                sp.wait_ge(h_done.sem, h_done.done(DEPTH - 1, 3 * KT + m))
                sp.dma_start(y[:, m, :], h[:, m, :]).then_inc(y_out, 16)
            sp.wait_ge(y_out, 16 * KT)

        @block.tensor
        def _(pe):
            for e in (*job_done.values(), stat_ps, z_ss, v_turned, scored, turned, weighed, proj_done):
                e.open(pe)
            pe.wait_ge(const_in, 16)

            def ready(s, l, k):
                pe.wait_ge(lo_made[s].sem, lo_made[s].done(l, k))
                pe.wait_ge(emptied[s].sem, emptied[s].done(l, k - 1))

            def products(out, hi_w, lo_w, hi, lo, first, last):
                mm = None
                for n, (w, a) in enumerate(((hi_w, hi), (hi_w, lo), (lo_w, hi))):
                    for (c0, c1), cols in zip(CHUNKS, a):
                        mm = nc.tensor.matmul(ps[out][:, c0:c1], w, cols, start=first and n == 0,
                                              stop=last and n == 2)
                return mm

            def piece(s, kt, out, hi, lo, first, last):
                return products(out, w_hi[s][:, kt, :], w_lo[s][:, kt, :], hi, lo, first, last)

            def cols(t, kt):
                return t[:, kt, 0:SEQ], t[:, kt, SEQ:T]

            def act_cols(t, kt):
                return t[:, kt, C_PROMPT], t[:, kt, C_SAMPLE]

            def in_piece(s, kt):
                return piece(s, kt, s, cols(in_hi, kt), cols(in_lo, kt), kt == 0, kt == KT - 1)

            def in_job(s, l, k, phase=None, between=None):
                ready(s, l, k)
                for kt in range(KT):
                    if phase is not None:
                        pe.wait_ge(in_lo_made.sem, in_lo_made.done(l, phase * KT + kt))
                    mm = in_piece(s, kt)
                    if between and between[0] == kt:
                        between[1](l)
                mm.then_inc(job_done[s].sem, 1)

            def stat(l, n, out, sums, w=ones):
                for c0, c1 in CHUNKS:
                    mm = nc.tensor.matmul(ps[out][:, c0:c1], w, sums[:, c0:c1], start=True, stop=True)
                return mm

            def head_squares(l, r):
                pe.wait_ge(z_sq.sem, z_sq.done(l, r))
                pe.wait_ge(z_root.sem, z_root.done(l, r - 1))
                stat(l, r, "C", zsq, head_ones).then_inc(z_ss.sem, 1)

            def turn_v(l):
                pe.wait_ge(emptied["B"].sem, emptied["B"].done(l, 2))
                for t in range(T // P):
                    mm = nc.tensor.transpose(ps["D"][:, t * P:(t + 1) * P], z[1][:, t * P:(t + 1) * P], ident)
                mm.then_inc(v_turned.sem, 1)

            def scores(l, n):
                head, q0, k0, nk = unit_of(n)
                if n % 6 == 0:
                    pe.wait_ge(qk_placed.sem, qk_placed.done(l, 8 + 4 * (n // 6 + 1) - 1))
                for t in range(2):
                    pe.wait_ge(exped.sem, exped.done(l, 2 * (n - 1) + t))
                    q = q_st[:, head, q0 + t * P:q0 + (t + 1) * P]
                    out = ps["C"][:, t * 512:t * 512 + nk]
                    nc.tensor.matmul(out, q, k_hi[:, head // Q_PER_KV, k0:k0 + nk], start=True, stop=False)
                    nc.tensor.matmul(out, q, k_lo[:, head // Q_PER_KV, k0:k0 + nk], start=False,
                                     stop=True).then_inc(scored.sem, 1)

            def turn(l, n, t):
                nk = unit_of(n)[3]
                pe.wait_ge(normed.sem, normed.done(l, 2 * n + t))
                pe.wait_ge(pt_lo_made.sem, pt_lo_made.done(l, 2 * n + t - 1))
                for b in range(nk // P):
                    mm = nc.tensor.transpose(ps["D"][:, b * P:(b + 1) * P],
                                             probs[:, n % 2, t, b * P:(b + 1) * P], ident)
                mm.then_inc(turned.sem, 1)

            def weigh(l, n):
                head, _, k0, nk = unit_of(n)
                pe.wait_ge(pt_lo_made.sem, pt_lo_made.done(l, 2 * n + 1))
                pe.wait_ge(o_out.sem, o_out.done(l, n - 1))
                nb = nk // P
                for b in range(nb):
                    v = v_hl[:, k0 // P + b, head // Q_PER_KV, :]
                    nc.tensor.matmul(ps["D"][:, 512:512 + UQ], v, pt_hi[:, b, :], start=b == 0, stop=False)
                    mm = nc.tensor.matmul(ps["D"][:, 512:512 + UQ], v, pt_lo[:, b, :], start=False,
                                          stop=b == nb - 1)
                mm.then_inc(weighed.sem, 1)

            with pe.Fori(0, DEPTH) as l:
                def input_stat(l):
                    pe.wait_ge(summed.sem, summed.done(l, -1))
                    stat(l, 0, "C", sum_h).then_inc(stat_ps.sem, 1)

                in_job("A", l, 0, phase=0, between=(6, input_stat))
                pe.wait_ge(stat_root.sem, stat_root.done(l, 0))
                for r in range(5):
                    in_job(*slot_of(r + 1)[:1], l, slot_of(r + 1)[1], between=(2, lambda l, r=r: head_squares(l, r)))

                in_job("A", l, AT_MIX, between=(2, turn_v))
                pe.wait_ge(z_root.sem, z_root.done(l, 4))
                pe.wait_ge(v_lo.sem, v_lo.done(l, 0))
                left_over = iter([(*mix_job(q), kt) for q in range(1, N_MIX) for kt in range(KT)])

                def next_piece():
                    s, k, kt = next(left_over)
                    if kt == 0:
                        ready(s, l, k)
                    mm = in_piece(s, kt)
                    if kt == KT - 1:
                        mm.then_inc(job_done[s].sem, 1)

                scores(l, 0)
                for n in range(N_UNITS):
                    turn(l, n, 0)
                    if n + 1 < N_UNITS:
                        scores(l, n + 1)
                    next_piece()
                    turn(l, n, 1)
                    next_piece()
                    if PIECES[n] == 4:
                        next_piece()
                    weigh(l, n)
                    next_piece()

                def out_job(s, k, order, first=False):
                    ready(s, l, k)
                    attn_ps, conv_ps = ("A", "B") if s == "A" else ("C", "D")
                    for n, kt in enumerate(order):
                        if first:
                            pe.wait_ge(mix_lo_made.sem, mix_lo_made.done(l, n))
                        mm = piece(s, kt, conv_ps if kt >= 4 else attn_ps, cols(mix_hi, kt), cols(mix_lo, kt),
                                   kt % 4 == 0, kt % 4 == 3)
                    mm.then_inc(job_done[s].sem, 1)

                pe.wait_ge(emptied["B"].sem, emptied["B"].done(l, AT_OUT - 1))
                out_job("A", AT_OUT, MIX_ORDER, first=True)
                pe.wait_ge(summed.sem, summed.done(l, 8))
                stat(l, 1, "C", sum_h).then_inc(stat_ps.sem, 1)
                pe.wait_ge(summed.sem, summed.done(l, 9))
                stat(l, 2, "D", sum_c).then_inc(stat_ps.sem, 1)
                pe.wait_ge(stat_root.sem, stat_root.done(l, 2))
                out_job("B", AT_OUT, range(KT))
                with pe.Fori(1, 4) as i:
                    out_job("A", AT_OUT + i, range(KT))
                    out_job("B", AT_OUT + i, range(KT))

                for f in range(HALVES):
                    if f == 0:
                        in_job("A", l, AT_UP[0], phase=1)
                        pe.wait_ge(summed.sem, summed.done(l, 18))
                        pe.wait_ge(emptied["B"].sem, emptied["B"].done(l, AT_OUT + 3))
                        stat(l, 3, "C", sum_h).then_inc(stat_ps.sem, 1)
                        in_job("B", l, AT_UP[0])
                    with pe.Fori(1 if f == 0 else 0, HALF) as i:
                        in_job("A", l, AT_UP[f] + i)
                        in_job("B", l, AT_UP[f] + i)
                    def down_job(s, k, first=False):
                        ready(s, l, k)
                        for kt in range(HALF):
                            if first:
                                pe.wait_ge(act_lo_made.sem, act_lo_made.done(l, f * HALF + kt))
                            mm = piece(s, kt, s, act_cols(act_hi, kt), act_cols(act_lo, kt), kt == 0, kt == HALF - 1)
                        mm.then_inc(job_done[s].sem, 1)

                    down_job("A", AT_DOWN[f], first=True)
                    down_job("B", AT_DOWN[f])
                    with pe.Fori(1, 4) as i:
                        down_job("A", AT_DOWN[f] + i)
                        down_job("B", AT_DOWN[f] + i)

                def proj_job(m):
                    out = "CD"[m % 2]
                    if m >= 2:
                        pe.wait_ge(p_gated.sem, p_gated.done(l, m - 2))
                    for kt in range(KT_PLE):
                        w = slice((m * KT_PLE + kt) * P, (m * KT_PLE + kt + 1) * P)
                        a = [[t[:, kt * T + c0:kt * T + c1] for c0, c1 in CHUNKS] for t in (p_hi, p_lo)]
                        mm = products(out, proj_hi[:, w], proj_lo[:, w], *a, kt == 0, kt == KT_PLE - 1)
                    mm.then_inc(proj_done.sem, 1)

                in_job("A", l, AT_PLE, phase=2)
                in_job("B", l, AT_PLE)
                pe.wait_ge(proj_lo_made.sem, proj_lo_made.done(l, 0))
                for m in range(8):
                    proj_job(m)
                    if m + 2 < 8:
                        in_job("AB"[m % 2], l, AT_PLE + (m + 2) // 2)

        @block.scalar
        def _(act):
            for e in (*hi_made.values(), in_hi_made, mix_hi_made, z_sq, proj_hi_made, stat_root, z_root, z_hi, v_hi, centre, exped, pt_hi_made,
                      o_low_out, *up_centre, silued, act_hi_made, p_hi_made, sigmoided):
                e.open(act)
            for t in range(KT):
                act.wait_ge(x_in[t], 16)
                if t >= 2:
                    act.wait_ge(x_sum, t)
                nc.scalar.activation((zsq, zrot)[t % 2][:], h[:, t, :], ACT.Square).then_inc(x_sq, 1)
            act.dma_start(cos_sin[:], tables).then_inc(tables_in, 16)
            act.wait_ge(eps_set, 1)

            def w_high(s, l, k, kt):
                act.wait_ge(raw_in[s].sem, raw_in[s].done(l, k))
                act.wait_ge(job_done[s].sem, job_done[s].done(l, k - 1))
                nc.scalar.copy(w_hi[s][:, 0:kt, :].rearrange("p k n -> p (k n)"),
                               raw[s][:, 0:kt * P]).then_inc(hi_made[s].sem, 1)

            def root(out, src, n):
                return nc.scalar.activation(out, src, ACT.Sqrt, bias=eps[:, 0:1], scale=1.0 / n)

            def z_roots(l, r):
                act.wait_ge(z_ss.sem, z_ss.done(l, r))
                root(zsq[:], ps["C"][:, 0:T], HEAD_DIM).then_inc(z_root.sem, 1)

            def z_high(l, r):
                act.wait_ge(z_roped.sem, z_roped.done(l, r))
                act.wait_ge(qk_placed.sem, qk_placed.done(l, (8 + 4 * (r - 1) if r else 0) - 1))
                nc.scalar.copy(qk_hi[:], zcos[:, 0:T]).then_inc(z_hi.sem, 1)

            def z_square(l, r):
                s, k = slot_of(r)
                act.wait_ge(emptied[s].sem, emptied[s].done(l, k))
                act.wait_ge(z_scaled.sem, z_scaled.done(l, r - 1))
                nc.scalar.activation(zsq[:], z[r % 2][:], ACT.Square).then_inc(z_sq.sem, 1)

            with act.Fori(0, DEPTH) as l:
                w_high("A", l, 0, KT)
                act.wait_ge(vec_set.sem, vec_set.done(l, 0))
                act.wait_ge(h_done.sem, h_done.done(l, -1))
                for s in "AB":
                    act.wait_ge(job_done[s].sem, job_done[s].done(l, -1))
                for t in range(KT):
                    nc.scalar.activation(in_hi[:, t, :], h[:, t, :], ACT.Copy,
                                         scale=vc[:, V_ATTN + t:V_ATTN + t + 1]).then_inc(in_hi_made.sem, 1)
                    if t == 1:
                        w_high("B", l, 0, KT)
                act.wait_ge(stat_ps.sem, stat_ps.done(l, 0))
                root(r_in[:], ps["C"][:, 0:T], D_MODEL).then_inc(stat_root.sem, 1)
                for r in range(6):
                    w_high(*slot_of(r + 2)[:1], l, slot_of(r + 2)[1], KT)
                    if r < 5:
                        z_square(l, r)
                    if r > 0:
                        z_high(l, r - 1)
                    if r < 5:
                        z_roots(l, r)
                act.wait_ge(v_turned.sem, v_turned.done(l, 0))
                nc.scalar.copy(v_hl[:, :, :, 0:64],
                               ps["D"][:, 0:T].rearrange("p (t g d) -> p t g d", g=N_KV, d=HEAD_DIM)
                               ).then_inc(v_hi.sem, 1)
                w_high("A", l, AT_MIX + 1, KT)

                def exp(n, t):
                    nk = unit_of(n)[3]
                    act.wait_ge(neg_topped.sem, neg_topped.done(l, 2 * n + t))
                    if n >= 2:
                        act.wait_ge(turned.sem, turned.done(l, 2 * (n - 2) + t))
                    c = 2 * (n % 2) + t
                    nc.scalar.activation(probs[:, n % 2, t, 0:nk], ps["C"][:, t * 512:t * 512 + nk], ACT.Exp,
                                         bias=neg_top[:, c:c + 1], scale=SCALE,
                                         accum_out=total[:, c:c + 1]).then_inc(exped.sem, 1)

                def pt_high(n, t):
                    nb = unit_of(n)[3] // P
                    act.wait_ge(turned.sem, turned.done(l, 2 * n + t))
                    act.wait_ge(weighed.sem, weighed.done(l, n - 1))
                    nc.scalar.copy(pt_hi[:, 0:nb, t * P:(t + 1) * P],
                                   ps["D"][:, 0:nb * P].rearrange("p (b q) -> p b q", q=P)
                                   ).then_inc(pt_hi_made.sem, 1)

                def mixer_centre(j):
                    act.wait_ge(gated.sem, gated.done(l, j))
                    nc.scalar.activation(conv_out[:], conv_in[:, 1:1 + CW], ACT.Copy,
                                         scale=vc[:, V_MCONV + 4 + j:V_MCONV + 5 + j]).then_inc(centre.sem, 1)

                act.wait_ge(z_lo.sem, z_lo.done(l, 4))
                act.wait_ge(qk_placed.sem, qk_placed.done(l, 23))
                exp(0, 0)
                exp(0, 1)
                for n in range(N_UNITS):
                    pt_high(n, 0)
                    if n + 1 < N_UNITS:
                        exp(n + 1, 0)
                    pt_high(n, 1)
                    if n + 1 < N_UNITS:
                        exp(n + 1, 1)
                    act.wait_ge(weighed.sem, weighed.done(l, n))
                    act.wait_ge(o_out.sem, o_out.done(l, n - 1))
                    nc.scalar.copy(o_low[:], ps["D"][64:128, 512:512 + UQ]).then_inc(o_low_out.sem, 1)
                    for q in ENDS[n]:
                        s, k = mix_job(q + 2)
                        w_high(s, l, k, KT)
                        if q % 3 == 2 and q < N_MIX - 1:
                            mixer_centre(q // 3)

                act.wait_ge(o_out.sem, o_out.done(l, N_UNITS - 1))
                for n, t in enumerate(MIX_ORDER):
                    if n == 2:
                        mixer_centre(3)
                    if t == 7:
                        act.wait_ge(mixed.sem, mixed.done(l, 3))
                    nc.scalar.activation(mix_hi[:, t, :], mix[:, t, :], ACT.Copy,
                                         scale=vc[:, V_MIX + t:V_MIX + t + 1]).then_inc(mix_hi_made.sem, 1)
                act.wait_ge(stat_ps.sem, stat_ps.done(l, 1))
                root(r_attn[:], ps["C"][:, 0:T], ATTN_W).then_inc(stat_root.sem, 1)
                act.wait_ge(stat_ps.sem, stat_ps.done(l, 2))
                root(r_conv[:], ps["D"][:, 0:T], CONV_W).then_inc(stat_root.sem, 1)

                def ffn_input(m):
                    act.wait_ge(h_done.sem, h_done.done(l, m))
                    nc.scalar.activation(in_hi[:, bass.ds(m, 1), :].rearrange("p a t -> p (a t)"),
                                         h[:, bass.ds(m, 1), :].rearrange("p a t -> p (a t)"), ACT.Copy,
                                         scale=vc[:, bass.ds(V_FFN + m, 1)]).then_inc(in_hi_made.sem, 1)

                with act.Fori(0, 3) as i:
                    w_high("A", l, AT_OUT + i + 1, KT)
                    ffn_input(2 * i)
                    w_high("B", l, AT_OUT + i + 1, KT)
                    ffn_input(2 * i + 1)
                w_high("A", l, AT_UP[0], KT)
                ffn_input(6)
                w_high("B", l, AT_UP[0], KT)
                ffn_input(7)

                def up_centre_tap(i, n, side):
                    act.wait_ge(emptied["AB"[side]].sem, emptied["AB"[side]].done(l, AT_UP[n] + i))
                    act.wait_ge(product.sem, product.done(l, n * HALF + i - 1))
                    if side:
                        act.wait_ge(act_lo_made.sem, act_lo_made.done(l, n * HALF + i - 1))
                    c = V_FCONV + 2 * FF_TILES + side * FF_TILES + n * HALF
                    nc.scalar.activation(up_out[side], up_in[side][:, 1:1 + CW], ACT.Copy,
                                         scale=vc[:, bass.ds(c + i, 1)]).then_inc(up_centre[side].sem, 1)

                def ffn_pair(f, i, kt, k_a, k_b):
                    w_high("A", l, k_a, kt)
                    if isinstance(i, int) and i == 0 and f == 0:
                        act.wait_ge(stat_ps.sem, stat_ps.done(l, 3))
                        root(r_in[:], ps["C"][:, 0:T], D_MODEL).then_inc(stat_root.sem, 1)
                    up_centre_tap(i, f, 0)
                    act.wait_ge(up_right[0].sem, up_right[0].done(l, f * HALF + i))
                    nc.scalar.activation(up_out[0], up_out[0], ACT.Silu).then_inc(silued.sem, 1)
                    w_high("B", l, k_b, kt)
                    up_centre_tap(i, f, 1)
                    act.wait_ge(product.sem, product.done(l, f * HALF + i))
                    if isinstance(i, int) and i == 0:
                        act.wait_ge(job_done["A"].sem, job_done["A"].done(l, AT_UP[f] - 1))
                        act.wait_ge(job_done["B"].sem, job_done["B"].done(l, AT_UP[f] - 1))
                    nc.scalar.copy(act_hi[:, bass.ds(i, 1), :].rearrange("p a c -> p (a c)"),
                                   up_out[1]).then_inc(act_hi_made.sem, 1)

                for f in range(HALVES):
                    ffn_pair(f, 0, KT, AT_UP[f] + 1, AT_UP[f] + 1)
                    with act.Fori(1, HALF - 1) as i:
                        ffn_pair(f, i, KT, AT_UP[f] + i + 1, AT_UP[f] + i + 1)
                    ffn_pair(f, HALF - 1, HALF, AT_DOWN[f], AT_DOWN[f])
                    def ple_input(m):
                        if f == 1:
                            act.wait_ge(h_done.sem, h_done.done(l, 2 * KT + m))
                            nc.scalar.copy(in_hi[:, bass.ds(m, 1), :].rearrange("p a t -> p (a t)"),
                                           h[:, bass.ds(m, 1), :].rearrange("p a t -> p (a t)")
                                           ).then_inc(in_hi_made.sem, 1)

                    with act.Fori(0, 3) as i:
                        w_high("A", l, AT_DOWN[f] + i + 1, HALF)
                        ple_input(2 * i)
                        w_high("B", l, AT_DOWN[f] + i + 1, HALF)
                        ple_input(2 * i + 1)
                    w_high("A", l, AT_DOWN[f] + 4, KT)
                    ple_input(6)
                    w_high("B", l, AT_DOWN[f] + 4, KT)
                    ple_input(7)

                act.wait_ge(p_in.sem, p_in.done(l, 0))
                nc.scalar.copy(p_hi[:], p_raw).then_inc(p_hi_made.sem, 1)
                act.wait_ge(proj_in.sem, proj_in.done(l, 0))
                nc.scalar.copy(proj_hi[:], proj_raw).then_inc(proj_hi_made.sem, 1)
                for m in range(8):
                    s, k = "AB"[m % 2], AT_PLE + m // 2
                    if m + 2 < 8:
                        w_high(s, l, k + 1, KT)
                    act.wait_ge(job_done[s].sem, job_done[s].done(l, k))
                    if m >= 2:
                        act.wait_ge(p_gated.sem, p_gated.done(l, m - 2))
                    nc.scalar.activation(gate[m % 2][:], ps[s][:, 0:T], ACT.Sigmoid).then_inc(sigmoided.sem, 1)

        @block.gpsimd
        def _(pool):
            for e in (*lo_made.values(), squared, z_cos, product):
                e.open(pool)
            nc.gpsimd.memset(eps[:], EPS).then_inc(eps_set, 1)

            def w_low(s, l, k, kt):
                pool.wait_ge(hi_made[s].sem, hi_made[s].done(l, k))
                nc.gpsimd.tensor_tensor(w_lo[s][:, 0:kt, :].rearrange("p k n -> p (k n)"), raw[s][:, 0:kt * P],
                                        w_hi[s][:, 0:kt, :].rearrange("p k n -> p (k n)").bitcast(F32),
                                        ALU.subtract).then_inc(lo_made[s].sem, 1)

            def add_square(l, k, src, acc, into):
                pool.wait_ge(summed.sem, summed.done(l, into - 1))
                nc.gpsimd.tensor_tensor(sq[:], src, src, ALU.mult).then_inc(squared.sem, 1)
                pool.wait_ge(squared.sem, squared.done(l, k))
                nc.gpsimd.tensor_tensor(acc[:], acc[:], sq[:], ALU.add).then_inc(summed.sem, 1)

            def z_cosine(l, r):
                pool.wait_ge(z_scaled.sem, z_scaled.done(l, r))
                pool.wait_ge(z_hi.sem, z_hi.done(l, r - 1))
                pool.wait_ge(z_lo.sem, z_lo.done(l, r - 1))
                nc.gpsimd.tensor_tensor(zcos[:, 0:T], z[r % 2][:], cos_sin[:, 0, :], ALU.mult).then_inc(z_cos.sem, 1)

            pool.wait_ge(tables_in, 16)
            with pool.Fori(0, DEPTH) as l:
                w_low("A", l, 0, KT)
                w_low("B", l, 0, KT)
                for r in range(6):
                    w_low(*slot_of(r + 2)[:1], l, slot_of(r + 2)[1], KT)
                    if r < 5:
                        z_cosine(l, r)
                w_low("A", l, AT_MIX + 1, KT)

                pool.wait_ge(stat_ps.sem, stat_ps.done(l, 0))
                pool.sem_inc(settled["pool"], 1)
                nc.gpsimd.memset(sum_h[:], 0.0).then_inc(summed.sem, 1)
                nc.gpsimd.memset(sum_c[:], 0.0).then_inc(summed.sem, 1)
                for n in range(N_UNITS):
                    for q in ENDS[n]:
                        s, k = mix_job(q + 2)
                        w_low(s, l, k, KT)
                    if n % 6 == 5:
                        j = n // 6
                        pool.wait_ge(o_out.sem, o_out.done(l, n))
                        add_square(l, 2 * j, mix[:, j, :], sum_h, 2 + 2 * j)
                        pool.wait_ge(mixed.sem, mixed.done(l, j))
                        add_square(l, 2 * j + 1, mix[:, 4 + j, :], sum_c, 3 + 2 * j)

                pool.wait_ge(stat_ps.sem, stat_ps.done(l, 2))
                pool.sem_inc(settled["pool"], 1)
                nc.gpsimd.memset(sum_h[:], 0.0).then_inc(summed.sem, 1)

                def out_squares(m):
                    pool.wait_ge(h_done.sem, h_done.done(l, m))
                    add_square(l, 8 + m, h[:, bass.ds(m, 1), :].rearrange("p a t -> p (a t)"), sum_h, 11 + m)

                with pool.Fori(0, 3) as i:
                    w_low("A", l, AT_OUT + i + 1, KT)
                    out_squares(2 * i)
                    w_low("B", l, AT_OUT + i + 1, KT)
                    out_squares(2 * i + 1)
                w_low("A", l, AT_UP[0], KT)
                out_squares(6)
                w_low("B", l, AT_UP[0], KT)
                out_squares(7)

                def multiply(f, i):
                    pool.wait_ge(silued.sem, silued.done(l, f * HALF + i))
                    pool.wait_ge(up_right[1].sem, up_right[1].done(l, f * HALF + i))
                    nc.gpsimd.tensor_tensor(up_out[1], up_out[0], up_out[1], ALU.mult).then_inc(product.sem, 1)

                for f in range(HALVES):
                    with pool.Fori(0, HALF - 1) as i:
                        w_low("A", l, AT_UP[f] + i + 1, KT)
                        w_low("B", l, AT_UP[f] + i + 1, KT)
                        multiply(f, i)
                    w_low("A", l, AT_DOWN[f], HALF)
                    w_low("B", l, AT_DOWN[f], HALF)
                    multiply(f, HALF - 1)
                    with pool.Fori(0, 3) as i:
                        w_low("A", l, AT_DOWN[f] + i + 1, HALF)
                        w_low("B", l, AT_DOWN[f] + i + 1, HALF)
                    w_low("A", l, AT_DOWN[f] + 4, KT)
                    w_low("B", l, AT_DOWN[f] + 4, KT)

                pool.wait_ge(stat_ps.sem, stat_ps.done(l, 3))
                pool.sem_inc(settled["pool"], 1)
                nc.gpsimd.memset(sum_h[:], 0.0).then_inc(summed.sem, 1)

                def ple_squares(m):
                    pool.wait_ge(h_done.sem, h_done.done(l, 3 * KT + m))
                    add_square(l, 16 + m, h[:, bass.ds(m, 1), :].rearrange("p a t -> p (a t)"), sum_h, 20 + m)

                for m in range(8):
                    if m + 2 < 8:
                        w_low("AB"[m % 2], l, AT_PLE + m // 2 + 1, KT)
                    ple_squares(m)

        @block.vector
        def _(dve):
            for e in (*emptied.values(), in_lo_made, stat_ready, z_inv, z_scaled, z_sin, z_roped, z_lo,
                      v_lo, padded, gated, left, right, mixed, topped, neg_topped, inverted, normed, pt_lo_made,
                      o_out, *scaled.values(), added, *up_left, *up_right, act_lo_made, p_lo_made, mix_lo_made, proj_lo_made, p_gated):
                e.open(dve)
            nc.vector.memset(sum_h[:], 0.0).then_inc(x_sum, 1)
            for t in range(KT):
                dve.wait_ge(x_sq, t + 1)
                dve.wait_ge(x_sum, t + 1)
                nc.vector.tensor_tensor(sum_h[:], sum_h[:], (zsq, zrot)[t % 2][:], ALU.add).then_inc(
                    summed.sem if t == KT - 1 else x_sum, 1)
            dve.wait_ge(summed.sem, 1)
            h_done.open(dve)
            dve.wait_ge(tables_in, 16)

            def low(made, k, dst, src, hi, gain=None):
                dve.wait_ge(made[0].sem, made[0].done(*k))
                if gain is None:
                    ins = nc.vector.tensor_tensor(dst, src, hi.bitcast(F32), ALU.subtract)
                else:
                    ins = nc.vector.scalar_tensor_tensor(dst, src, gain, hi.bitcast(F32), ALU.mult, ALU.subtract)
                ins.then_inc(made[1].sem, 1)

            in_made, mix_made = (in_hi_made, in_lo_made), (mix_hi_made, mix_lo_made)

            def tile_of(t, m):
                return t[:, bass.ds(m, 1), :].rearrange("p a t -> p (a t)")

            def recip(l, n, r):
                dve.wait_ge(stat_root.sem, stat_root.done(l, n))
                nc.vector.reciprocal(r[:], r[:]).then_inc(stat_ready.sem, 1)

            def pads(l, k, bufs):
                ins = None
                for b in bufs:
                    for c in PADS:
                        ins = nc.vector.memset(b[:, c], 0.0)
                ins.then_inc(padded.sem, 1)

            def empty(s, l, k, out):
                dve.wait_ge(job_done[s].sem, job_done[s].done(l, k))
                if out.shape[-1] == UW:
                    nc.vector.tensor_tensor(out[:, U_PROMPT], ps[s][:, 0:SEQ], r_in[:, 0:SEQ], ALU.mult)
                    ins = nc.vector.tensor_tensor(out[:, U_SAMPLE], ps[s][:, SEQ:T], r_in[:, SEQ:T], ALU.mult)
                else:
                    ins = nc.vector.tensor_tensor(out, ps[s][:, 0:T], r_in[:], ALU.mult)
                ins.then_inc(emptied[s].sem, 1)

            def z_scale(l, r):
                dve.wait_ge(z_root.sem, z_root.done(l, r))
                nc.vector.reciprocal(zsq[:], zsq[:]).then_inc(z_inv.sem, 1)
                dve.wait_ge(z_inv.sem, z_inv.done(l, r))
                gain = V_QG if r else V_KG
                nc.vector.scalar_tensor_tensor(z[r % 2][:], z[r % 2][:], vc[:, gain:gain + 1], zsq[:],
                                               ALU.mult, ALU.mult).then_inc(z_scaled.sem, 1)

            def z_rope(l, r):
                dve.wait_ge(z_swapped.sem, z_swapped.done(l, 4 * r + 3))
                nc.vector.tensor_tensor(zrot[:], zrot[:], cos_sin[:, 1, :], ALU.mult).then_inc(z_sin.sem, 1)
                dve.wait_ge(z_sin.sem, z_sin.done(l, r))
                dve.wait_ge(z_cos.sem, z_cos.done(l, r))
                nc.vector.tensor_tensor(zcos[:, 0:T], zcos[:, 0:T], zrot[:], ALU.add).then_inc(z_roped.sem, 1)
                dve.wait_ge(z_hi.sem, z_hi.done(l, r))
                nc.vector.tensor_tensor(qk_lo[:], zcos[:, 0:T], qk_hi[:].bitcast(F32), ALU.subtract).then_inc(z_lo.sem, 1)

            with dve.Fori(0, DEPTH) as l:
                dve.wait_ge(vec_set.sem, vec_set.done(l, 0))
                for t in range(KT):
                    low(in_made, (l, t), in_lo[:, t, :], h[:, t, :], in_hi[:, t, :],
                        vc[:, V_ATTN + t:V_ATTN + t + 1])
                recip(l, 0, r_in)
                dve.wait_ge(stat_ready.sem, stat_ready.done(l, 0))
                for r in range(6):
                    if r >= 2:
                        dve.wait_ge(z_cos.sem, z_cos.done(l, r - 2))
                        dve.wait_ge(z_swapped.sem, z_swapped.done(l, 4 * (r - 2) + 3))
                    empty(*slot_of(r)[:1], l, slot_of(r)[1], z[r % 2][:])
                    if r > 0:
                        z_rope(l, r - 1)
                    if r < 5:
                        z_scale(l, r)
                dve.wait_ge(v_hi.sem, v_hi.done(l, 0))
                nc.vector.tensor_tensor(v_hl[:, :, :, 64:128],
                                        ps["D"][:, 0:T].rearrange("p (t g d) -> p t g d", g=N_KV, d=HEAD_DIM),
                                        v_hl[:, :, :, 0:64].bitcast(F32), ALU.subtract).then_inc(v_lo.sem, 1)
                pads(l, 0, [conv_in])
                dve.wait_ge(padded.sem, padded.done(l, 0))

                def top_of(n, t):
                    nk, c = unit_of(n)[3], 2 * (n % 2) + t
                    dve.wait_ge(scored.sem, scored.done(l, 2 * n + t))
                    nc.vector.reduce_max(top[:, c:c + 1], ps["C"][:, t * 512:t * 512 + nk], AX_X).then_inc(topped.sem, 1)
                    dve.wait_ge(topped.sem, topped.done(l, 2 * n + t))
                    nc.vector.tensor_scalar(neg_top[:, c:c + 1], top[:, c:c + 1], -SCALE, None,
                                            ALU.mult).then_inc(neg_topped.sem, 1)

                def norm(n, t):
                    nk, c = unit_of(n)[3], 2 * (n % 2) + t
                    dve.wait_ge(exped.sem, exped.done(l, 2 * n + t))
                    nc.vector.reciprocal(inv_total[:, c:c + 1], total[:, c:c + 1]).then_inc(inverted.sem, 1)
                    dve.wait_ge(inverted.sem, inverted.done(l, 2 * n + t))
                    a = probs[:, n % 2, t, 0:nk]
                    nc.vector.tensor_scalar(a, a, inv_total[:, c:c + 1], None, ALU.mult).then_inc(normed.sem, 1)

                def pt_low(n, t):
                    nb = unit_of(n)[3] // P
                    dve.wait_ge(pt_hi_made.sem, pt_hi_made.done(l, 2 * n + t))
                    nc.vector.tensor_tensor(pt_lo[:, 0:nb, t * P:(t + 1) * P],
                                            ps["D"][:, 0:nb * P].rearrange("p (b q) -> p b q", q=P),
                                            pt_hi[:, 0:nb, t * P:(t + 1) * P].bitcast(F32),
                                            ALU.subtract).then_inc(pt_lo_made.sem, 1)

                def mixer(q):
                    (s, k), (j, part) = mix_job(q), divmod(q, 3)
                    if part == 0:
                        empty(s, l, k, mix[:, 4 + j, :])
                    elif part == 1:
                        empty(s, l, k, conv_in)
                    else:
                        empty(s, l, k, conv_out[:, 0:T])
                        dve.wait_ge(emptied[s].sem, emptied[s].done(l, k))
                        before = mix_job(q - 1)
                        dve.wait_ge(emptied[before[0]].sem, emptied[before[0]].done(l, before[1]))
                        nc.vector.tensor_tensor(conv_in[:, U_PROMPT], conv_in[:, U_PROMPT], conv_out[:, 0:SEQ],
                                                ALU.mult)
                        nc.vector.tensor_tensor(conv_in[:, U_SAMPLE], conv_in[:, U_SAMPLE], conv_out[:, SEQ:T],
                                                ALU.mult).then_inc(gated.sem, 1)

                def mixer_taps(j):
                    dve.wait_ge(centre.sem, centre.done(l, j))
                    c = V_MCONV + j
                    nc.vector.scalar_tensor_tensor(conv_out[:], conv_in[:, 0:CW], vc[:, c:c + 1], conv_out[:],
                                                   ALU.mult, ALU.add).then_inc(left.sem, 1)
                    dve.wait_ge(left.sem, left.done(l, j))
                    nc.vector.scalar_tensor_tensor(conv_out[:], conv_in[:, 2:2 + CW], vc[:, c + 8:c + 9], conv_out[:],
                                                   ALU.mult, ALU.add).then_inc(right.sem, 1)
                    dve.wait_ge(right.sem, right.done(l, j))
                    gb = mix[:, 4 + j, :]
                    nc.vector.tensor_tensor(gb[:, 0:SEQ], gb[:, 0:SEQ], conv_out[:, C_PROMPT], ALU.mult)
                    nc.vector.tensor_tensor(gb[:, SEQ:T], gb[:, SEQ:T], conv_out[:, C_SAMPLE],
                                            ALU.mult).then_inc(mixed.sem, 1)

                mixer(0)
                for t in range(2):
                    top_of(0, t)
                for t in range(2):
                    norm(0, t)
                taps_left = []
                for n in range(N_UNITS):
                    pt_low(n, 0)
                    if n + 1 < N_UNITS:
                        top_of(n + 1, 0)
                        top_of(n + 1, 1)
                    pt_low(n, 1)
                    if n + 1 < N_UNITS:
                        norm(n + 1, 0)
                        norm(n + 1, 1)
                    head, q0 = unit_of(n)[:2]
                    dve.wait_ge(o_low_out.sem, o_low_out.done(l, n))
                    r = 64 * (head % 2)
                    nc.vector.tensor_tensor(mix[r:r + 64, head // 2, q0:q0 + UQ], ps["D"][0:64, 512:512 + UQ],
                                            o_low[:], ALU.add).then_inc(o_out.sem, 1)
                    for j in taps_left:
                        mixer_taps(j)
                    taps_left = []
                    for q in ENDS[n]:
                        mixer(q)
                        taps_left += [q // 3] if q % 3 == 2 else []

                for n, t in enumerate(MIX_ORDER):
                    if n == 2:
                        mixer_taps(3)
                    low(mix_made, (l, n), mix_lo[:, t, :], mix[:, t, :], mix_hi[:, t, :],
                        vc[:, V_MIX + t:V_MIX + t + 1])
                recip(l, 1, r_attn)
                recip(l, 2, r_conv)
                dve.wait_ge(stat_ready.sem, stat_ready.done(l, 2))
                dve.sem_inc(settled["dve"], 1)
                t_conv, t_attn = conv_in[:, 0:T], conv_out[:, 0:T]

                def out_tile(s, k, m):
                    attn_ps, conv_ps = ("A", "B") if s == "A" else ("C", "D")
                    dve.wait_ge(job_done[s].sem, job_done[s].done(l, k))
                    dve.wait_ge(h_done.sem, h_done.done(l, m - 1))
                    nc.vector.tensor_tensor(t_conv, ps[conv_ps][:, 0:T], r_conv[:], ALU.mult).then_inc(
                        scaled["conv"].sem, 1)
                    nc.vector.tensor_tensor(t_attn, ps[attn_ps][:, 0:T], r_attn[:], ALU.mult).then_inc(
                        emptied[s].sem, 1)
                    dve.wait_ge(scaled["conv"].sem, scaled["conv"].done(l, m))
                    dst = h[:, bass.ds(m, 1), :].rearrange("p a t -> p (a t)")
                    nc.vector.tensor_tensor(dst, dst, t_conv, ALU.add).then_inc(added.sem, 1)
                    dve.wait_ge(added.sem, added.done(l, m))
                    dve.wait_ge(emptied[s].sem, emptied[s].done(l, k))
                    nc.vector.tensor_tensor(dst, dst, t_attn, ALU.add).then_inc(h_done.sem, 1)

                    low(in_made, (l, KT + m), tile_of(in_lo, m), dst, tile_of(in_hi, m),
                        vc[:, bass.ds(V_FFN + m, 1)])

                with dve.Fori(0, 4) as i:
                    out_tile("A", AT_OUT + i, 2 * i)
                    out_tile("B", AT_OUT + i, 2 * i + 1)

                pads(l, 1, up_in)
                recip(l, 3, r_in)
                dve.wait_ge(stat_ready.sem, stat_ready.done(l, 3))

                def up_taps(f, i, side):
                    n = f * HALF + i
                    dve.wait_ge(up_centre[side].sem, up_centre[side].done(l, n))
                    c = V_FCONV + side * FF_TILES + f * HALF
                    out = up_out[side]
                    nc.vector.scalar_tensor_tensor(out, up_in[side][:, 0:CW], vc[:, bass.ds(c + i, 1)], out,
                                                   ALU.mult, ALU.add).then_inc(up_left[side].sem, 1)
                    dve.wait_ge(up_left[side].sem, up_left[side].done(l, n))
                    nc.vector.scalar_tensor_tensor(out, up_in[side][:, 2:2 + CW],
                                                   vc[:, bass.ds(c + 4 * FF_TILES + i, 1)], out,
                                                   ALU.mult, ALU.add).then_inc(up_right[side].sem, 1)

                def ffn_pair(f, i):
                    dve.wait_ge(up_right[0].sem, up_right[0].done(l, f * HALF + i - 1))
                    empty("A", l, AT_UP[f] + i, up_in[0])
                    up_taps(f, i, 0)
                    dve.wait_ge(up_right[1].sem, up_right[1].done(l, f * HALF + i - 1))
                    empty("B", l, AT_UP[f] + i, up_in[1])
                    up_taps(f, i, 1)
                    dve.wait_ge(act_hi_made.sem, act_hi_made.done(l, f * HALF + i))
                    dst = act_lo[:, bass.ds(i, 1), :].rearrange("p a c -> p (a c)")
                    hi = act_hi[:, bass.ds(i, 1), :].rearrange("p a c -> p (a c)").bitcast(F32)
                    nc.vector.tensor_tensor(dst, up_out[1], hi, ALU.subtract).then_inc(act_lo_made.sem, 1)

                def down_tile(s, k, f, m):
                    dve.wait_ge(job_done[s].sem, job_done[s].done(l, k))
                    dst = h[:, bass.ds(m, 1), :].rearrange("p a t -> p (a t)")
                    nc.vector.tensor_tensor(dst, ps[s][:, 0:T], dst, ALU.add).then_inc(h_done.sem, 1)
                    dve.wait_ge(h_done.sem, h_done.done(l, (1 + f) * KT + m))
                    emptied[s].open(dve)
                    if f == 1:
                        low(in_made, (l, 2 * KT + m), tile_of(in_lo, m), dst, tile_of(in_hi, m))

                dve.wait_ge(padded.sem, padded.done(l, 1))
                dve.sem_inc(settled["dve"], 1)
                for f in range(HALVES):
                    with dve.Fori(0, HALF) as i:
                        ffn_pair(f, i)
                    with dve.Fori(0, 4) as i:
                        down_tile("A", AT_DOWN[f] + i, f, 2 * i)
                        down_tile("B", AT_DOWN[f] + i, f, 2 * i + 1)

                dve.wait_ge(p_hi_made.sem, p_hi_made.done(l, 0))
                nc.vector.tensor_tensor(p_lo[:], p_raw, p_hi[:].bitcast(F32), ALU.subtract).then_inc(p_lo_made.sem, 1)
                dve.wait_ge(proj_hi_made.sem, proj_hi_made.done(l, 0))
                nc.vector.tensor_tensor(proj_lo[:], proj_raw, proj_hi[:].bitcast(F32),
                                        ALU.subtract).then_inc(proj_lo_made.sem, 1)
                for m in range(8):
                    s = "AB"[m % 2]
                    dve.wait_ge(sigmoided.sem, sigmoided.done(l, m))
                    emptied[s].open(dve)
                    dve.wait_ge(proj_done.sem, proj_done.done(l, m))
                    if m >= 2:
                        dve.wait_ge(h_done.sem, h_done.done(l, 3 * KT + m - 2))
                    nc.vector.tensor_tensor(gated_p[m % 2][:], ps["CD"[m % 2]][:, 0:T], gate[m % 2][:],
                                            ALU.mult).then_inc(p_gated.sem, 1)
                    dve.wait_ge(p_gated.sem, p_gated.done(l, m))
                    nc.vector.tensor_tensor(h[:, m, :], h[:, m, :], gated_p[m % 2][:],
                                            ALU.add).then_inc(h_done.sem, 1)


def _weight_tiles(w, kt):
    depth, _, cols = w.shape
    a = w.reshape(depth, kt, P, cols // P, P).transpose(0, 3, 2, 1, 4)
    return a.reshape(depth * (cols // P), P, kt * P)


def _rope_tables():
    half = HEAD_DIM // 2
    freqs = np.float32(ROPE_THETA) ** (-np.arange(0, half, 2, dtype=np.float32) / np.float32(half))
    pos = np.arange(SEQ)
    row, col = (pos // GRID_W).astype(np.float32), (pos % GRID_W).astype(np.float32)
    ang = np.concatenate([row[:, None] * freqs, row[:, None] * freqs,
                          col[:, None] * freqs, col[:, None] * freqs], axis=1)
    sign = np.repeat(np.array([-1, 1, -1, 1], np.float32), HEAD_DIM // 4)
    cos, sin = np.cos(ang).T[ROPE_ORDER], (np.sin(ang) * sign).T[ROPE_ORDER]
    both = [np.tile(np.concatenate([t, t[:, :DEC_SEQ]], axis=1), (2, 1)) for t in (cos, sin)]
    return np.ascontiguousarray(np.stack(both, axis=1), dtype=np.float32)


def kernel(**inputs):
    import concourse.bacc as bacc
    from concourse.bass_utils import run_bass_kernel_spmd

    a = {k: np.asarray(v) for k, v in inputs.items()}

    def channels(prompt, sample, n):
        both = np.concatenate([prompt, sample], axis=0).T
        return both.reshape(n, P, T).transpose(1, 0, 2)

    def columns(v):
        return v.reshape(-1, P).T

    vec = []
    for l in range(DEPTH):
        vec.append(np.concatenate([columns(a["attn_norm_g"][l]), columns(a["ffn_norm_g"][l]), columns(a["attn_out_g"][l]),
                columns(a["conv_out_g"][l]), np.tile(a["q_norm_g"][l][ROPE_ORDER], 2)[:, None],
                np.tile(a["k_norm_g"][l][ROPE_ORDER], 2)[:, None], columns(a["mix_conv_w"][l]), columns(a["ffn_conv_w"][l])], axis=1))
    qk_w = ATTN_W + N_KV * HEAD_DIM
    in_order = [HEAD_DIM * head + c for head in range(qk_w // HEAD_DIM) for c in ROPE_ORDER]
    in_order += range(qk_w, D_IN)
    eye = np.eye(P, dtype=np.float32)
    heads = np.kron(np.eye(2, dtype=np.float32), np.ones((HEAD_DIM, HEAD_DIM), np.float32))
    w_down = a["w_down"].reshape(DEPTH * HALVES, HALF * P, D_MODEL)
    arrays = {
        "x": channels(a["x_prompt"][0], a["x_sample"][0], KT),
        "p": np.stack([channels(a["p_prompt"][l, 0], a["p_sample"][l, 0], KT_PLE).reshape(P, KT_PLE * T)
                       for l in range(DEPTH)]),
        "w_in": _weight_tiles(a["w_in"][:, :, in_order], KT), "w_out": _weight_tiles(a["w_out"], KT),
        "w_up": _weight_tiles(a["w_up"], KT), "w_down": _weight_tiles(w_down, HALF),
        "w_gate": _weight_tiles(a["w_ple_gate"], KT), "w_proj": _weight_tiles(a["w_ple_proj"], KT_PLE).reshape(DEPTH, 8, P, KT_PLE * P).transpose(0, 2, 1, 3)
        .reshape(DEPTH, P, 8 * KT_PLE * P),
        "vec": np.stack(vec), "tables": _rope_tables(),
        "mats": np.stack([eye, np.ones((P, P), np.float32), heads], axis=1),
    }
    nc = bacc.Bacc("TRN2", target_bir_lowering=False, num_devices=1, dynamic_dma_scratch_size=1024)
    arrays = {f"in_{k}": np.ascontiguousarray(v) for k, v in arrays.items()}
    args = [nc.dram_tensor(k, v.shape, F32, kind="ExternalInput").ap() for k, v in arrays.items()]
    y = nc.dram_tensor("out_y", (P, KT, T), F32, kind="ExternalOutput").ap()
    trunk_program(nc, *args, y)
    r = run_bass_kernel_spmd(nc, [arrays], core_ids=[0])
    out = r.results[0]["out_y"].transpose(1, 0, 2).reshape(D_MODEL, T).T
    return (np.ascontiguousarray(out[:SEQ])[None], np.ascontiguousarray(out[SEQ:])[None])
```

```python
from contextlib import ExitStack

import numpy as np

import concourse.bass as bass
from concourse import mybir

F32 = mybir.dt.float32
F32R = mybir.dt.float32r
ALU = mybir.AluOpType
ACT = mybir.ActivationFunctionType
AX_X = mybir.AxisListType.X

P = 128
DEPTH, D_MODEL, SEQ, DEC_SEQ = 2, 1024, 512, 256
T = SEQ + DEC_SEQ
HEAD_DIM, N_HEADS, N_KV = 64, 8, 2
Q_PER_KV = N_HEADS // N_KV
ATTN_W, CONV_W, D_FF, PLE_DIM = 512, 512, 2816, 256
D_IN = ATTN_W + 2 * N_KV * HEAD_DIM + 3 * CONV_W
GRID_W, ROPE_THETA, EPS = 64, 10000.0, 1e-6
SCALE = HEAD_DIM ** -0.5

KT = D_MODEL // P
IN_TILES = D_IN // P
FF_TILES = D_FF // P
HALVES = 2
HALF = FF_TILES // HALVES
KT_PLE = PLE_DIM // P
CHUNKS = ((0, SEQ), (SEQ, T))

UW = T + 4
CW = T + 2
U_PROMPT, U_SAMPLE = slice(1, 1 + SEQ), slice(SEQ + 3, SEQ + 3 + DEC_SEQ)
C_PROMPT, C_SAMPLE = slice(0, SEQ), slice(SEQ + 2, CW)
PADS = (slice(0, 1), slice(SEQ + 1, SEQ + 3), slice(UW - 1, UW))

IN_ORDER = [4, 0, 1, 2, 3, 5] + [t + j for j in range(4) for t in (10, 14, 6)]
N_QKV, N_MIX = 6, 12

ROPE_ORDER = [16 * b + i for b in (0, 2, 1, 3) for i in range(16)]

AT_QKV, AT_MIX = 0, N_QKV // 2
AT_OUT = AT_MIX + N_MIX // 2
AT_UP = [AT_OUT + 4, AT_OUT + 4 + HALF + 4]
AT_DOWN = [a + HALF for a in AT_UP]
AT_PLE = AT_DOWN[1] + 4
N_USES = AT_PLE + 4

V_ATTN, V_FFN, V_MIX, V_QG, V_KG, V_MCONV = 0, 8, 16, 24, 25, 26
V_FCONV = V_MCONV + 3 * 4
N_VEC = V_FCONV + 3 * 2 * FF_TILES

NF = 2 * T // P
F_HI, F_LO = slice(0, NF), slice(32, 32 + NF)
F_IN, F_HEADS, F_ATTN, F_CONV, F_FFN = 0, 1, 6, 7, 8

UNITS = ((0, 0, SEQ), (256, 0, SEQ), (SEQ, SEQ, DEC_SEQ))
UQ = 256
N_UNITS = N_HEADS * len(UNITS)

MIX_ORDER = (0, 1, 2, 4, 5, 6, 3, 7)
PIECES = [3 if n % 3 == 2 else 4 for n in range(N_UNITS)]
PIECES[15], PIECES[-1] = PIECES[15] - 1, PIECES[-1] + 1
ENDS = [[q for q in range(1, N_MIX) if sum(PIECES[:n]) < KT * q <= sum(PIECES[:n + 1])] for n in range(N_UNITS)]
assert sum(PIECES) == KT * (N_MIX - 1)
STEP_LAGS = ((2, 3, 5, 7), (1, 2, 4, 6), (1, 2, 4, 6), (1, 2))
U_ENDS = [n for n in range(N_UNITS) for q in ENDS[n] if q % 3 == 1]
MIX_STEPS = [[(step, j) for j, lags in enumerate(STEP_LAGS) for step, lag in enumerate(lags) if U_ENDS[j] + lag == n]
             for n in range(N_UNITS)]
SQUARE_AT = {U_ENDS[j] + STEP_LAGS[j][3] + 1: j for j in range(3)}


def slot_of(g):
    return "AB"[g % 2], g // 2


def mix_job(q):
    return slot_of(N_QKV + q)


IN_ADDED = ((2, 4, 6, 7), (3, 5))


class Event:

    def __init__(self, sem, per_layer, by=1, ahead=0):
        self.sem, self.per_layer, self.by, self.ahead = sem, per_layer, by, ahead

    def done(self, layer, k):
        return (layer * self.per_layer + k + 2 + self.ahead) * self.by

    def open(self, eng):
        eng.sem_inc(self.sem, self.by * (1 + self.ahead))


def trunk_program(nc, x, p, w_in, w_out, w_up, w_down, w_gate, w_proj, vec, tables, mats, spread_of, y):
    with ExitStack() as ctx:
        def sb(name, shape, dt=F32, where=ctx):
            return where.enter_context(nc.sbuf_tensor(name, shape, dt))

        def event(name, per_layer, by=1, ahead=0):
            return Event(ctx.enter_context(nc.semaphore(name)), per_layer, by, ahead)

        h = sb("h", [P, KT, T])
        in_hi, in_lo = sb("in_hi", [P, KT, T], F32R), sb("in_lo", [P, KT, T], F32R)
        raw = {s: sb(f"raw{s}", [P, HALF * P]) for s in "AB"}
        w_hi = {s: sb(f"w_hi{s}", [P, HALF, P], F32R) for s in "AB"}
        w_lo = {s: sb(f"w_lo{s}", [P, HALF, P], F32R) for s in "AB"}
        mix = sb("mix", [P, KT, T])
        mix_flat = mix[:].rearrange("p k t -> p (k t)")
        conv_in, conv_out = sb("conv_in", [P, UW]), sb("conv_out", [P, CW])
        cos_sin = sb("cos_sin", [P, 2, T])
        r_in = sb("r_in", [P, T])
        sum_h = sb("sum_h", [P, T])
        mat = sb("mat", [P, P + 4])
        ident, all_cols, head_cols = mat[:, 0:P], mat[:, P:P + 2], mat[:, P + 2:P + 4]
        spread = sb("spread", [F_LO.stop, T], F32R)
        f_root, f_inv = ([sb(f"{n}{i}", [P, NF]) for i in range(2)] for n in ("f_root", "f_inv"))
        f_hl = [sb(f"f_hl{i}", [F_LO.stop, P], F32R) for i in range(2)]
        vc = sb("vc", [P, N_VEC])
        eps = sb("eps", [P, 1])
        top, neg_top, total, inv_total = (sb(n, [P, 4]) for n in ("top", "neg_top", "total", "inv_total"))
        with ExitStack() as att:
            q_st = sb("q_st", [P, N_HEADS, T], F32R, att)
            k_hi, k_lo = sb("k_hi", [P, N_KV, T], F32R, att), sb("k_lo", [P, N_KV, T], F32R, att)
            v_hl = sb("v_hl", [P, T // P, N_KV, 2 * HEAD_DIM], F32R, att)
            qk_hi = sb("qk_hi", [P, T], F32R, att)
            pt_hi = sb("pt_hi", [P, SEQ // P, UQ], F32R, att)
            pt_lo = sb("pt_lo", [P, SEQ // P, UQ], F32R, att)
            probs = sb("probs", [P, 2, 2, SEQ], F32, att)
            o_low = sb("o_low", [HEAD_DIM, UQ], F32, att)
            sq = sb("sq", [P, T], F32, att)
            with ExitStack() as sums:
                sum_c = sb("sum_c", [P, T], F32, sums)
            qk_lo = sb("qk_lo", [P, T], F32R, att)
        with ExitStack() as out:
            mix_hi, mix_lo = sb("mix_hi", [P, KT, T], F32R, out), sb("mix_lo", [P, KT, T], F32R, out)
        with ExitStack() as ple:
            p_hi, p_lo = sb("p_hi", [P, KT_PLE * T], F32R, ple), sb("p_lo", [P, KT_PLE * T], F32R, ple)
            proj_hi = sb("proj_hi", [P, 8 * KT_PLE * P], F32R, ple)
            proj_lo = sb("proj_lo", [P, 8 * KT_PLE * P], F32R, ple)
            gate = [sb(f"gate{i}", [P, T], F32, ple) for i in range(8)]
        act_hi, act_lo = sb("act_hi", [P, HALF, CW], F32R), sb("act_lo", [P, HALF, CW], F32R)
        z, zsq, zrot = [mix[:, 5 + i, :] for i in range(3)], mix[:, 3, :], [mix[:, 1 + i, :] for i in range(2)]
        squares = (sq[:], zsq)
        zcos = (conv_out[:, 0:T], conv_in[:, 0:T])
        up_in = [mix_flat[:, i * UW:(i + 1) * UW] for i in range(2)]
        up_out = [mix_flat[:, 2 * UW + i * CW:2 * UW + (i + 1) * CW] for i in range(2)]
        p_raw = mix_flat[:, 2 * UW + 2 * CW:2 * UW + 2 * CW + KT_PLE * T]
        r_attn, r_conv = mix_flat[:, 0:T], mix_flat[:, T:2 * T]
        proj_raw = mix_flat[:, 0:8 * KT_PLE * P]

        ps = {n: ctx.enter_context(nc.psum_tensor(f"ps{n}", [P, 1024], F32)) for n in "ABCD"}

        raw_in = {s: event(f"raw_in_{s}", N_USES, 16) for s in "AB"}
        hi_made = {s: event(f"hi_made_{s}", N_USES) for s in "AB"}
        lo_made = {s: event(f"lo_made_{s}", N_USES) for s in "AB"}
        job_done = {s: event(f"job_done_{s}", N_USES) for s in "AB"}
        emptied = {s: event(f"emptied_{s}", N_USES) for s in "AB"}
        vec_set = event("vec_set", 1, 16)
        in_hi_made, in_lo_made = event("in_hi_made", 3 * KT), event("in_lo_made", 3 * KT)
        mix_hi_made, mix_lo_made = event("mix_hi_made", KT), event("mix_lo_made", KT)
        h_done = event("h_done", 3 * KT)
        h_next = [event(f"h_next{i}", KT // 2, ahead=KT // 2) for i in range(2)]
        in_sq = event("in_sq", KT)
        in_sum = [event(f"in_sum{i}", len(IN_ADDED[i])) for i in range(2)]
        squared, summed = event("squared", 8), event("summed", 10)
        h_squared, h_summed = event("h_squared", KT), event("h_summed", KT - 1)
        f_summed, f_rooted, f_inverted, f_turned, f_hi_made, f_lo_made, f_spread = (
            event(n, 9) for n in ("f_summed", "f_rooted", "f_inverted", "f_turned", "f_hi_made", "f_lo_made",
                                  "f_spread"))
        r_copied = event("r_copied", 4)
        z_sq, z_scaled = event("z_sq", 5), event("z_scaled", 5)
        z_swapped = event("z_swapped0", 12, 16), event("z_swapped1", 8, 16)
        z_cos, z_sin, z_roped = event("z_cos", 5), event("z_sin", 5), event("z_roped", 5)
        z_hi, z_lo = event("z_hi", 5), event("z_lo", 5)
        qk_placed = event("qk_placed", 8 + 4 * 4, 16)
        v_turned, v_hi, v_lo = event("v_turned", 1), event("v_hi", 1), event("v_lo", 1)
        padded = event("padded", 2)
        gated, centre, left, right, mixed = (event(n, 4) for n in ("gated", "centre", "left", "right", "mixed"))
        nq = 2 * N_UNITS
        scored, topped, neg_topped, exped = (event(n, nq) for n in ("scored", "topped", "neg_topped", "exped"))
        inverted, normed, turned, pt_hi_made, pt_lo_made = (
            event(n, nq) for n in ("inverted", "normed", "turned", "pt_hi_made", "pt_lo_made"))
        weighed, o_low_out, o_out = (event(n, N_UNITS) for n in ("weighed", "o_low_out", "o_out"))
        scaled = {"attn": event("scaled_attn", 8)}
        added = event("added", 8)
        up_centre = [event(f"up_centre{i}", FF_TILES) for i in range(2)]
        up_left = [event(f"up_left{i}", FF_TILES) for i in range(2)]
        up_right = [event(f"up_right{i}", FF_TILES) for i in range(2)]
        silued, product = event("silued", FF_TILES), event("product", FF_TILES)
        act_hi_made, act_lo_made = event("act_hi_made", FF_TILES), event("act_lo_made", FF_TILES)
        p_in, p_hi_made, p_lo_made = event("p_in", 1, 16), event("p_hi_made", 1), event("p_lo_made", 1)
        proj_in, proj_hi_made, proj_lo_made = event("proj_in", 1, 16), event("proj_hi_made", 1), event("proj_lo_made", 1)
        proj_done, p_gated = event("proj_done", 8), event("p_gated", 8)
        const_in = ctx.enter_context(nc.semaphore("const_in"))
        x_in = [ctx.enter_context(nc.semaphore(f"x_in{n}")) for n in range(KT // 2)]
        spread_set = ctx.enter_context(nc.semaphore("spread_set"))
        tables_in = ctx.enter_context(nc.semaphore("tables_in"))
        first_issued = ctx.enter_context(nc.semaphore("first_issued"))
        eps_set = ctx.enter_context(nc.semaphore("eps_set"))
        y_out = ctx.enter_context(nc.semaphore("y_out"))

        settled = {e: ctx.enter_context(nc.semaphore(f"settled_{e}")) for e in ("act", "pool", "dve", "sp")}

        def unit_of(n):
            return (n // 3,) + UNITS[n % 3]

        def steps_of(n):
            return [(0, 1), (1, 1)] if unit_of(n)[3] == SEQ else [(0, 2)]

        def both(ap, tiles, nb):
            return ap.rearrange("p (t b q) -> p t b q", t=tiles, b=nb)

        block = ctx.enter_context(nc.Block())

        @block.sync
        def _(sp):
            for e in (*raw_in.values(), vec_set, *z_swapped, qk_placed, p_in, proj_in):
                e.open(sp)
            sp.dma_start(zrot[0][0:F_LO.stop, :], spread_of).then_inc(spread_set, 16)
            sp.dma_start(h[:, 0:2, :], x[:, 0:2, :]).then_inc(x_in[0], 16)

            def load(s, l, k, src, kt):
                w, tile = src
                at = sp.snap(tile)
                sp.wait_ge(lo_made[s].sem, lo_made[s].done(l, k - 1))
                sp.dma_start(raw[s][:, 0:kt * P], w[at]).then_inc(raw_in[s].sem, 16)

            def swap(l, r):
                sp.wait_ge(z_scaled.sem, z_scaled.done(l, r))
                sp.sem_inc(settled["sp"], 1)
                sp.wait_ge(z_roped.sem, z_roped.done(l, r - 2))
                for to, of in ((0, 32), (32, 0), (64, 96), (96, 64)):
                    sp.dma_start(zrot[r % 2][to:to + 32, :], z[r % 3][of:of + 32, :]).then_inc(z_swapped[r % 2].sem, 16)

            def place_k(l):
                sp.wait_ge(z_lo.sem, z_lo.done(l, 0))
                for g in range(N_KV):
                    for half in range(2):
                        rows = slice(half * 64, half * 64 + 64)
                        for dst, src in ((k_hi, qk_hi), (k_lo, qk_lo)):
                            sp.dma_start(dst[rows, g, :].bitcast(F32), src[g * 64:g * 64 + 64, :].bitcast(F32)).then_inc(qk_placed.sem, 16)

            def place_q(l, j):
                sp.wait_ge(z_lo.sem, z_lo.done(l, j + 1))
                for hh in range(2):
                    for half, src in enumerate((qk_hi, qk_lo)):
                        sp.dma_start(q_st[half * 64:half * 64 + 64, 2 * j + hh, :].bitcast(F32),
                                     src[hh * 64:hh * 64 + 64, :].bitcast(F32)).then_inc(qk_placed.sem, 16)

            with sp.Fori(0, DEPTH) as l:
                def w_in_load(g):
                    s, k = slot_of(g)
                    load(s, l, k, (w_in, l * IN_TILES + IN_ORDER[g]), KT)

                layer = sp.snap(l)
                sp.wait_ge(act_lo_made.sem, act_lo_made.done(l, -1))
                sp.dma_start(vc[:], vec[layer]).then_inc(vec_set.sem, 16)
                w_in_load(0)
                sp.sem_inc(first_issued, 1)
                for g in range(1, 4):
                    w_in_load(g)
                w_in_load(4)
                swap(l, 0)
                w_in_load(5)
                for r in range(5):
                    if r < 4:
                        swap(l, r + 1)
                    if r == 0:
                        place_k(l)
                    else:
                        place_q(l, r - 1)
                    if r < 4:
                        w_in_load(6 + r)
                for g in range(10, N_QKV + N_MIX):
                    w_in_load(g)
                with sp.Fori(0, 4) as i:
                    load("A", l, AT_OUT + i, (w_out, l * 8 + 2 * i), KT)
                    load("B", l, AT_OUT + i, (w_out, l * 8 + 2 * i + 1), KT)
                layer = sp.snap(l)
                sp.wait_ge(mix_lo_made.sem, mix_lo_made.done(l, KT - 1))
                sp.dma_start(p_raw, p[layer]).then_inc(p_in.sem, 16)
                for f in range(HALVES):
                    with sp.Fori(0, HALF) as i:
                        load("A", l, AT_UP[f] + i, (w_up, l * 2 * FF_TILES + f * HALF + i), KT)
                        load("B", l, AT_UP[f] + i, (w_up, l * 2 * FF_TILES + FF_TILES + f * HALF + i), KT)
                    with sp.Fori(0, 4) as i:
                        load("A", l, AT_DOWN[f] + i, (w_down, (l * HALVES + f) * 8 + 2 * i), HALF)
                        load("B", l, AT_DOWN[f] + i, (w_down, (l * HALVES + f) * 8 + 2 * i + 1), HALF)
                    if f == 1:
                        layer = sp.snap(l)
                        sp.wait_ge(act_lo_made.sem, act_lo_made.done(l, FF_TILES - 1))
                        sp.dma_start(proj_raw, w_proj[layer]).then_inc(proj_in.sem, 16)
                with sp.Fori(0, 4) as i:
                    load("A", l, AT_PLE + i, (w_gate, l * 8 + 2 * i), KT)
                    load("B", l, AT_PLE + i, (w_gate, l * 8 + 2 * i + 1), KT)
            for m in range(KT):
                sp.wait_ge(h_next[m % 2].sem, h_next[m % 2].done(DEPTH - 1, m // 2))
                sp.dma_start(y[:, m, :], h[:, m, :]).then_inc(y_out, 16)
            sp.wait_ge(y_out, 16 * KT)

        @block.tensor
        def _(pe):
            for e in (*job_done.values(), f_summed, f_turned, f_spread, v_turned, scored, turned, weighed, proj_done):
                e.open(pe)

            def ready(s, l, k):
                pe.wait_ge(lo_made[s].sem, lo_made[s].done(l, k))
                pe.wait_ge(emptied[s].sem, emptied[s].done(l, k - 1))

            def products(out, hi_w, lo_w, hi, lo, first, last):
                mm = None
                for n, (w, a) in enumerate(((hi_w, hi), (hi_w, lo), (lo_w, hi))):
                    for (c0, c1), cols in zip(CHUNKS, a):
                        mm = nc.tensor.matmul(ps[out][:, c0:c1], w, cols, start=first and n == 0,
                                              stop=last and n == 2)
                return mm

            def piece(s, kt, out, hi, lo, first, last):
                return products(out, w_hi[s][:, kt, :], w_lo[s][:, kt, :], hi, lo, first, last)

            def cols(t, kt):
                return t[:, kt, 0:SEQ], t[:, kt, SEQ:T]

            def act_cols(t, kt):
                return t[:, kt, C_PROMPT], t[:, kt, C_SAMPLE]

            def in_piece(s, kt):
                return piece(s, kt, s, cols(in_hi, kt), cols(in_lo, kt), kt == 0, kt == KT - 1)

            def in_job(s, l, k, phase=None, between={}):
                ready(s, l, k)
                for kt in range(KT):
                    if phase is not None:
                        pe.wait_ge(in_lo_made.sem, in_lo_made.done(l, phase * KT + kt))
                    mm = in_piece(s, kt)
                    if kt in between:
                        between[kt]()
                mm.then_inc(job_done[s].sem, 1)

            def factor_sums(l, bank, squares, by=all_cols, start=True, stop=True):
                for t in range(T // P):
                    mm = nc.tensor.matmul(ps[bank][:, T + 2 * t:T + 2 * t + 2], squares[:, t * P:(t + 1) * P], by,
                                          start=start and t == 0, stop=stop and t == T // P - 1)
                return mm

            def factor_turn(l, f, bank):
                pe.wait_ge(f_inverted.sem, f_inverted.done(l, f))
                nc.tensor.transpose(ps[bank][0:NF, T + 16:T + 16 + P], f_inv[f % 2][:], ident).then_inc(f_turned.sem, 1)

            def factor_spread(l, f, bank):
                pe.wait_ge(f_lo_made.sem, f_lo_made.done(l, f))
                for t in range(T // P):
                    w, out = spread[:, t * P:(t + 1) * P], ps[bank][:, t * P:(t + 1) * P]
                    mm = nc.tensor.matmul(out, w, f_hl[f % 2][:], start=True, stop=True)
                mm.then_inc(f_spread.sem, 1)

            def head_factors(l, r, at):
                def sums():
                    pe.wait_ge(z_sq.sem, z_sq.done(l, r))
                    factor_sums(l, "CD"[r % 2], zsq, by=head_cols).then_inc(f_summed.sem, 1)

                def spread_out():
                    if r >= 2:
                        pe.wait_ge(z_scaled.sem, z_scaled.done(l, r - 2))
                    elif r == 0:
                        pe.wait_ge(r_copied.sem, r_copied.done(l, 0))
                    factor_spread(l, F_HEADS + r, "CD"[r % 2])

                return {at: sums, at + 1: lambda: factor_turn(l, F_HEADS + r, "CD"[r % 2]), at + 2: spread_out}

            def turn_v(l):
                pe.wait_ge(emptied["B"].sem, emptied["B"].done(l, 2))
                for t in range(T // P):
                    mm = nc.tensor.transpose(ps["D"][:, t * P:(t + 1) * P], z[2][:, t * P:(t + 1) * P], ident)
                mm.then_inc(v_turned.sem, 1)

            def scores(l, n):
                head, q0, k0, nk = unit_of(n)
                if n % 6 == 0:
                    pe.wait_ge(qk_placed.sem, qk_placed.done(l, 8 + 4 * (n // 6 + 1) - 1))
                for t in range(2):
                    pe.wait_ge(exped.sem, exped.done(l, 2 * (n - 1) + t))
                    q = q_st[:, head, q0 + t * P:q0 + (t + 1) * P]
                    out = ps["C"][:, t * 512:t * 512 + nk]
                    nc.tensor.matmul(out, q, k_hi[:, head // Q_PER_KV, k0:k0 + nk], start=True, stop=False)
                    nc.tensor.matmul(out, q, k_lo[:, head // Q_PER_KV, k0:k0 + nk], start=False,
                                     stop=True).then_inc(scored.sem, 1)

            def turn(l, n, t):
                nk = unit_of(n)[3]
                pe.wait_ge(normed.sem, normed.done(l, 2 * n + t))
                pe.wait_ge(pt_lo_made.sem, pt_lo_made.done(l, 2 * n + (t if nk == SEQ else 0) - 1))
                at = t * nk if nk < SEQ else 0
                for b in range(nk // P):
                    mm = nc.tensor.transpose(ps["D"][:, at + b * P:at + (b + 1) * P],
                                             probs[:, n % 2, t, b * P:(b + 1) * P], ident)
                mm.then_inc(turned.sem, 1)

            def weigh(l, n):
                head, _, k0, nk = unit_of(n)
                pe.wait_ge(pt_lo_made.sem, pt_lo_made.done(l, 2 * n + 1))
                pe.wait_ge(o_out.sem, o_out.done(l, n - 1))
                nb = nk // P
                for b in range(nb):
                    v = v_hl[:, k0 // P + b, head // Q_PER_KV, :]
                    nc.tensor.matmul(ps["D"][:, 512:512 + UQ], v, pt_hi[:, b, :], start=b == 0, stop=False)
                    mm = nc.tensor.matmul(ps["D"][:, 512:512 + UQ], v, pt_lo[:, b, :], start=False,
                                          stop=b == nb - 1)
                mm.then_inc(weighed.sem, 1)

            with pe.Fori(0, DEPTH) as l:
                def input_sums(i):
                    e = in_sum[1 - i]
                    pe.wait_ge(e.sem, e.done(l, len(IN_ADDED[1 - i]) - 1))
                    mm = factor_sums(l, "C", (sum_c, sum_h)[i], start=i == 0, stop=i == 1)
                    if i == 1:
                        mm.then_inc(f_summed.sem, 1)

                in_job("A", l, 0, phase=0)
                pe.wait_ge(const_in, 16)
                pe.wait_ge(spread_set, 17)
                in_job("B", l, 0, between={2: lambda: input_sums(0), 3: lambda: input_sums(1),
                                           4: lambda: factor_turn(l, F_IN, "C"),
                                           5: lambda: factor_spread(l, F_IN, "C")})
                in_job("A", l, 1, between={**head_factors(l, 0, 1), **head_factors(l, 1, 5)})
                for r, at in ((2, 3), (3, 4), (4, 2)):
                    s, k = slot_of(r + 1)
                    in_job(s, l, k, between=head_factors(l, r, at))

                def first_scores():
                    pe.wait_ge(z_scaled.sem, z_scaled.done(l, 4))
                    scores(l, 0)

                in_job("A", l, AT_MIX, between={3: first_scores, 5: lambda: turn_v(l)})
                pe.wait_ge(v_lo.sem, v_lo.done(l, 0))
                left_over = iter([(*mix_job(q), kt) for q in range(1, N_MIX) for kt in range(KT)])

                def next_piece():
                    s, k, kt = next(left_over)
                    if kt == 0:
                        ready(s, l, k)
                    mm = in_piece(s, kt)
                    if kt == KT - 1:
                        mm.then_inc(job_done[s].sem, 1)

                for n in range(N_UNITS):
                    short = unit_of(n)[3] < SEQ
                    turn(l, n, 0)
                    if short:
                        turn(l, n, 1)
                    if n + 1 < N_UNITS:
                        scores(l, n + 1)
                    next_piece()
                    if not short:
                        turn(l, n, 1)
                        next_piece()
                    next_piece()
                    weigh(l, n)
                    for _ in range(PIECES[n] - (2 if short else 3)):
                        next_piece()

                def out_job(s, k, order, first=False, between={}):
                    ready(s, l, k)
                    attn_ps, conv_ps = ("A", "B") if s == "A" else ("C", "D")
                    for n, kt in enumerate(order):
                        if first and kt == 4:
                            pe.wait_ge(emptied["B"].sem, emptied["B"].done(l, AT_OUT - 1))
                        if first:
                            pe.wait_ge(mix_lo_made.sem, mix_lo_made.done(l, n))
                        mm = piece(s, kt, conv_ps if kt >= 4 else attn_ps, cols(mix_hi, kt), cols(mix_lo, kt),
                                   kt % 4 == 0, kt % 4 == 3)
                        if n in between:
                            between[n]()
                    mm.then_inc(job_done[s].sem, 1)

                def attn_sums():
                    pe.wait_ge(summed.sem, summed.done(l, 8))
                    factor_sums(l, "C", sum_h).then_inc(f_summed.sem, 1)

                def conv_sums():
                    pe.wait_ge(summed.sem, summed.done(l, 9))
                    factor_sums(l, "D", sum_c).then_inc(f_summed.sem, 1)

                def bank_read(k):
                    pe.wait_ge(r_copied.sem, r_copied.done(l, k))

                out_job("A", AT_OUT, MIX_ORDER, first=True,
                        between={3: attn_sums, 5: lambda: factor_turn(l, F_ATTN, "C"),
                                 6: lambda: factor_spread(l, F_ATTN, "C")})
                bank_read(1)
                out_job("B", AT_OUT, range(KT), between={0: conv_sums, 1: lambda: factor_turn(l, F_CONV, "D"),
                                                         2: lambda: factor_spread(l, F_CONV, "D"),
                                                         3: lambda: bank_read(2)})
                with pe.Fori(1, 4) as i:
                    out_job("A", AT_OUT + i, range(KT))
                    out_job("B", AT_OUT + i, range(KT))

                for f in range(HALVES):
                    if f == 0:
                        def ffn_sums():
                            pe.wait_ge(h_summed.sem, h_summed.done(l, KT - 2))
                            pe.wait_ge(emptied["B"].sem, emptied["B"].done(l, AT_OUT + 3))
                            factor_sums(l, "C", sum_h).then_inc(f_summed.sem, 1)

                        in_job("A", l, AT_UP[0], phase=1)
                        in_job("B", l, AT_UP[0], between={0: ffn_sums, 1: lambda: factor_turn(l, F_FFN, "C"),
                                                          2: lambda: factor_spread(l, F_FFN, "C")})
                    with pe.Fori(1 if f == 0 else 0, HALF) as i:
                        in_job("A", l, AT_UP[f] + i)
                        in_job("B", l, AT_UP[f] + i)
                    def down_job(s, k, first=False):
                        ready(s, l, k)
                        for kt in range(HALF):
                            if first:
                                pe.wait_ge(act_lo_made.sem, act_lo_made.done(l, f * HALF + kt))
                            mm = piece(s, kt, s, act_cols(act_hi, kt), act_cols(act_lo, kt), kt == 0, kt == HALF - 1)
                        mm.then_inc(job_done[s].sem, 1)

                    down_job("A", AT_DOWN[f], first=True)
                    down_job("B", AT_DOWN[f])
                    with pe.Fori(1, 4) as i:
                        down_job("A", AT_DOWN[f] + i)
                        down_job("B", AT_DOWN[f] + i)

                def proj_job(m):
                    out = "CD"[m % 2]
                    if m >= 2:
                        pe.wait_ge(p_gated.sem, p_gated.done(l, m - 2))
                    for kt in range(KT_PLE):
                        w = slice((m * KT_PLE + kt) * P, (m * KT_PLE + kt + 1) * P)
                        a = [[t[:, kt * T + c0:kt * T + c1] for c0, c1 in CHUNKS] for t in (p_hi, p_lo)]
                        mm = products(out, proj_hi[:, w], proj_lo[:, w], *a, kt == 0, kt == KT_PLE - 1)
                    mm.then_inc(proj_done.sem, 1)

                in_job("A", l, AT_PLE, phase=2)
                in_job("B", l, AT_PLE)
                with pe.Fori(1, 4) as i:
                    in_job("A", l, AT_PLE + i)
                    in_job("B", l, AT_PLE + i)
                pe.wait_ge(proj_lo_made.sem, proj_lo_made.done(l, 0))
                for m in range(8):
                    proj_job(m)

        @block.scalar
        def _(act):
            for e in (*hi_made.values(), in_hi_made, mix_hi_made, z_sq, proj_hi_made, squared, h_squared, f_rooted, f_hi_made,
                      r_copied, z_hi, v_hi, centre, exped, pt_hi_made,
                      o_low_out, *up_centre, silued, act_hi_made, p_hi_made, in_sq):
                e.open(act)
            act.wait_ge(first_issued, 1)
            for n in range(1, KT // 2):
                act.dma_start(h[:, 2 * n:2 * n + 2, :], x[:, 2 * n:2 * n + 2, :]).then_inc(x_in[n], 16)
            act.dma_start(mat[:], mats).then_inc(const_in, 16)
            act.dma_start(cos_sin[:], tables).then_inc(tables_in, 16)
            act.wait_ge(eps_set, 1)

            def w_high(s, l, k, kt):
                act.wait_ge(raw_in[s].sem, raw_in[s].done(l, k))
                act.wait_ge(job_done[s].sem, job_done[s].done(l, k - 1))
                nc.scalar.copy(w_hi[s][:, 0:kt, :].rearrange("p k n -> p (k n)"),
                               raw[s][:, 0:kt * P]).then_inc(hi_made[s].sem, 1)

            def factor_root(l, f, bank, n):
                act.wait_ge(f_summed.sem, f_summed.done(l, f))
                if f >= 2:
                    act.wait_ge(f_inverted.sem, f_inverted.done(l, f - 2))
                nc.scalar.activation(f_root[f % 2][:], ps[bank][:, T:T + NF], ACT.Sqrt, bias=eps[:, 0:1],
                                     scale=1.0 / n).then_inc(f_rooted.sem, 1)

            def factor_high(l, f, bank):
                act.wait_ge(f_turned.sem, f_turned.done(l, f))
                if f >= 2:
                    act.wait_ge(f_spread.sem, f_spread.done(l, f - 2))
                nc.scalar.copy(f_hl[f % 2][F_HI, :], ps[bank][0:NF, T + 16:T + 16 + P]).then_inc(f_hi_made.sem, 1)

            def copy_factors(l, f, bank, out):
                act.wait_ge(f_spread.sem, f_spread.done(l, f))
                nc.scalar.copy(out, ps[bank][:, 0:T]).then_inc(r_copied.sem, 1)

            def square(l, k, src, after):
                act.wait_ge(summed.sem, summed.done(l, after))
                nc.scalar.activation(sq[:], src, ACT.Square).then_inc(squared.sem, 1)

            def square_h(l, m):
                if not (isinstance(m, int) and m == 0):
                    act.wait_ge(h_summed.sem, h_summed.done(l, m - 2))
                    act.sem_inc(settled["act"], 1)
                nc.scalar.activation((sum_h if isinstance(m, int) and m == 0 else sq)[:],
                                     h[:, bass.ds(m, 1), :].rearrange("p a t -> p (a t)"),
                                     ACT.Square).then_inc(h_squared.sem, 1)

            def z_high(l, r):
                act.wait_ge(z_roped.sem, z_roped.done(l, r))
                act.wait_ge(qk_placed.sem, qk_placed.done(l, (8 + 4 * (r - 1) if r else 0) - 1))
                nc.scalar.copy(qk_hi[:], zcos[r % 2]).then_inc(z_hi.sem, 1)

            def z_square(l, r):
                s, k = slot_of(r)
                act.wait_ge(emptied[s].sem, emptied[s].done(l, k))
                nc.scalar.activation(zsq, z[r % 3], ACT.Square).then_inc(z_sq.sem, 1)

            def square_in(l, t):
                out = (sum_h[:], sum_c[:])[t] if t < 2 else squares[t % 2]
                if t >= 4:
                    e = in_sum[t % 2]
                    act.wait_ge(e.sem, e.done(l, t // 2 - 2))
                nc.scalar.activation(out, h[:, t, :], ACT.Square).then_inc(in_sq.sem, 1)

            with act.Fori(0, DEPTH) as l:
                w_high("A", l, 0, KT)
                act.wait_ge(vec_set.sem, vec_set.done(l, 0))
                for s in "AB":
                    act.wait_ge(job_done[s].sem, job_done[s].done(l, -1))
                for t in range(KT):
                    act.wait_ge(x_in[t // 2], 16)
                    act.wait_ge(h_next[t % 2].sem, h_next[t % 2].done(l, t // 2 - KT // 2))
                    nc.scalar.activation(in_hi[:, t, :], h[:, t, :], ACT.Copy,
                                         scale=vc[:, V_ATTN + t:V_ATTN + t + 1]).then_inc(in_hi_made.sem, 1)
                    if t == 1:
                        w_high("B", l, 0, KT)
                    if t == 5:
                        square_in(l, 0)
                        square_in(l, 1)
                    if t == 6:
                        square_in(l, 2)
                for t in range(3, KT):
                    square_in(l, t)
                w_high("A", l, 1, KT)
                factor_root(l, F_IN, "C", D_MODEL)
                factor_high(l, F_IN, "C")
                copy_factors(l, F_IN, "C", r_in[:])

                def root(r):
                    factor_root(l, F_HEADS + r, "CD"[r % 2], HEAD_DIM)

                z_square(l, 0)
                w_high("B", l, 1, KT)
                root(0)
                z_square(l, 1)
                factor_high(l, F_HEADS + 0, "C")
                root(1)
                factor_high(l, F_HEADS + 1, "D")
                for r, before, after in ((2, (0,), ()), (3, (1,), ()), (4, (2,), (3,))):
                    s, k = slot_of(r + 2)
                    z_square(l, r)
                    w_high(s, l, k, KT)
                    for i in before:
                        z_high(l, i)
                    root(r)
                    factor_high(l, F_HEADS + r, "CD"[r % 2])
                    for i in after:
                        z_high(l, i)
                w_high("B", l, AT_MIX, KT)

                def exp(n, t):
                    nk = unit_of(n)[3]
                    act.wait_ge(neg_topped.sem, neg_topped.done(l, 2 * n + t))
                    if n >= 2:
                        act.wait_ge(turned.sem, turned.done(l, 2 * (n - 2) + t))
                    c = 2 * (n % 2) + t
                    nc.scalar.activation(probs[:, n % 2, t, 0:nk], ps["C"][:, t * 512:t * 512 + nk], ACT.Exp,
                                         bias=neg_top[:, c:c + 1], scale=SCALE,
                                         accum_out=total[:, c:c + 1]).then_inc(exped.sem, 1)

                def pt_high(n, t, tiles):
                    nb = unit_of(n)[3] // P
                    act.wait_ge(turned.sem, turned.done(l, 2 * n + t + tiles - 1))
                    act.wait_ge(weighed.sem, weighed.done(l, n - 1))
                    nc.scalar.copy(pt_hi[:, 0:nb, t * P:(t + tiles) * P].rearrange("p b (t q) -> p t b q", q=P),
                                   both(ps["D"][:, 0:tiles * nb * P], tiles, nb)).then_inc(pt_hi_made.sem, tiles)

                def mixer_high(n):
                    t = MIX_ORDER[n]
                    if t >= 4:
                        act.wait_ge(mixed.sem, mixed.done(l, t - 4))
                    nc.scalar.activation(mix_hi[:, t, :], mix[:, t, :], ACT.Copy,
                                         scale=vc[:, V_MIX + t:V_MIX + t + 1]).then_inc(mix_hi_made.sem, 1)

                def mixer_centre(j):
                    act.wait_ge(gated.sem, gated.done(l, j))
                    nc.scalar.activation(conv_out[:], conv_in[:, 1:1 + CW], ACT.Copy,
                                         scale=vc[:, V_MCONV + 4 + j:V_MCONV + 5 + j]).then_inc(centre.sem, 1)

                exp(0, 0)
                exp(0, 1)
                act.wait_ge(v_turned.sem, v_turned.done(l, 0))
                nc.scalar.copy(v_hl[:, :, :, 0:64],
                               ps["D"][:, 0:T].rearrange("p (t g d) -> p t g d", g=N_KV, d=HEAD_DIM)
                               ).then_inc(v_hi.sem, 1)
                w_high("A", l, AT_MIX + 1, KT)
                for n in range(N_UNITS):
                    for t, tiles in steps_of(n):
                        pt_high(n, t, tiles)
                    if n + 1 < N_UNITS:
                        exp(n + 1, 0)
                        exp(n + 1, 1)
                    for q in ENDS[n - 1] if n else []:
                        s, k = mix_job(q + 2)
                        w_high(s, l, k, KT)
                    if n == 1:
                        z_high(l, 4)
                    for step, j in MIX_STEPS[n]:
                        if step == 1:
                            mixer_centre(j)
                    if n % 6 == 1 and n > 6:
                        square(l, 2 * (n // 6 - 1), mix[:, n // 6 - 1, :], 1 + 2 * (n // 6 - 1))
                    j = SQUARE_AT.get(n)
                    if j is not None:
                        act.wait_ge(mixed.sem, mixed.done(l, j))
                        square(l, 2 * j + 1, mix[:, 4 + j, :], 2 + 2 * j)
                    if n >= N_UNITS - 5:
                        if n == N_UNITS - 5:
                            act.wait_ge(scored.sem, scored.done(l, 2 * 18 - 1))
                        mixer_high(n - (N_UNITS - 5))
                    act.wait_ge(weighed.sem, weighed.done(l, n))
                    act.wait_ge(o_out.sem, o_out.done(l, n - 1))
                    nc.scalar.copy(o_low[:], ps["D"][64:128, 512:512 + UQ]).then_inc(o_low_out.sem, 1)

                mixer_high(5)
                act.wait_ge(o_out.sem, o_out.done(l, N_UNITS - 1))
                mixer_high(6)
                square(l, 6, mix[:, 3, :], 7)
                s, k = mix_job(N_MIX + 1)
                w_high(s, l, k, KT)
                factor_root(l, F_ATTN, "C", ATTN_W)
                mixer_high(7)
                factor_high(l, F_ATTN, "C")
                square(l, 7, mix[:, 7, :], 8)
                copy_factors(l, F_ATTN, "C", r_attn)
                w_high("A", l, AT_OUT + 1, KT)
                factor_root(l, F_CONV, "D", CONV_W)
                factor_high(l, F_CONV, "D")
                copy_factors(l, F_CONV, "D", r_conv)

                def ffn_input(m):
                    act.wait_ge(h_done.sem, h_done.done(l, m))
                    nc.scalar.activation(in_hi[:, bass.ds(m, 1), :].rearrange("p a t -> p (a t)"),
                                         h[:, bass.ds(m, 1), :].rearrange("p a t -> p (a t)"), ACT.Copy,
                                         scale=vc[:, bass.ds(V_FFN + m, 1)]).then_inc(in_hi_made.sem, 1)

                def out_tile(m):
                    ffn_input(m)
                    square_h(l, m)

                out_tile(0)
                with act.Fori(0, 3) as i:
                    w_high("B", l, AT_OUT + i + 1, KT)
                    out_tile(2 * i + 1)
                    w_high("A", l, AT_OUT + i + 2, KT)
                    out_tile(2 * i + 2)
                w_high("B", l, AT_UP[0], KT)
                out_tile(7)

                def up_centre_tap(i, n, side):
                    act.wait_ge(emptied["AB"[side]].sem, emptied["AB"[side]].done(l, AT_UP[n] + i))
                    act.wait_ge(product.sem, product.done(l, n * HALF + i - 1))
                    if side:
                        act.wait_ge(act_lo_made.sem, act_lo_made.done(l, n * HALF + i - 1))
                    c = V_FCONV + 2 * FF_TILES + side * FF_TILES + n * HALF
                    nc.scalar.activation(up_out[side], up_in[side][:, 1:1 + CW], ACT.Copy,
                                         scale=vc[:, bass.ds(c + i, 1)]).then_inc(up_centre[side].sem, 1)

                def ffn_pair(f, i, kt, k_a, k_b):
                    w_high("A", l, k_a, kt)
                    if isinstance(i, int) and i == 0 and f == 0:
                        factor_root(l, F_FFN, "C", D_MODEL)
                        factor_high(l, F_FFN, "C")
                        copy_factors(l, F_FFN, "C", r_in[:])
                    up_centre_tap(i, f, 0)
                    act.wait_ge(up_right[0].sem, up_right[0].done(l, f * HALF + i))
                    nc.scalar.activation(up_out[0], up_out[0], ACT.Silu).then_inc(silued.sem, 1)
                    w_high("B", l, k_b, kt)
                    up_centre_tap(i, f, 1)
                    act.wait_ge(product.sem, product.done(l, f * HALF + i))
                    if isinstance(i, int) and i == 0:
                        act.wait_ge(job_done["A"].sem, job_done["A"].done(l, AT_UP[f] - 1))
                        act.wait_ge(job_done["B"].sem, job_done["B"].done(l, AT_UP[f] - 1))
                    nc.scalar.copy(act_hi[:, bass.ds(i, 1), :].rearrange("p a c -> p (a c)"),
                                   up_out[1]).then_inc(act_hi_made.sem, 1)

                for f in range(HALVES):
                    ffn_pair(f, 0, KT, AT_UP[f] + 1, AT_UP[f] + 1)
                    with act.Fori(1, HALF - 1) as i:
                        ffn_pair(f, i, KT, AT_UP[f] + i + 1, AT_UP[f] + i + 1)
                    ffn_pair(f, HALF - 1, HALF, AT_DOWN[f], AT_DOWN[f])
                    def ple_input(m):
                        if f == 1:
                            act.wait_ge(h_done.sem, h_done.done(l, 2 * KT + m))
                            nc.scalar.copy(in_hi[:, bass.ds(m, 1), :].rearrange("p a t -> p (a t)"),
                                           h[:, bass.ds(m, 1), :].rearrange("p a t -> p (a t)")
                                           ).then_inc(in_hi_made.sem, 1)

                    with act.Fori(0, 3) as i:
                        w_high("A", l, AT_DOWN[f] + i + 1, HALF)
                        ple_input(2 * i)
                        w_high("B", l, AT_DOWN[f] + i + 1, HALF)
                        ple_input(2 * i + 1)
                    w_high("A", l, AT_DOWN[f] + 4, KT)
                    ple_input(6)
                    w_high("B", l, AT_DOWN[f] + 4, KT)
                    ple_input(7)

                act.wait_ge(p_in.sem, p_in.done(l, 0))
                nc.scalar.copy(p_hi[:], p_raw).then_inc(p_hi_made.sem, 1)
                act.wait_ge(proj_in.sem, proj_in.done(l, 0))
                nc.scalar.copy(proj_hi[:], proj_raw).then_inc(proj_hi_made.sem, 1)
                for m in range(8):
                    s, k = "AB"[m % 2], AT_PLE + m // 2
                    if m + 2 < 8:
                        w_high(s, l, k + 1, KT)
                    act.wait_ge(job_done[s].sem, job_done[s].done(l, k))
                    nc.scalar.activation(gate[m][:], ps[s][:, 0:T], ACT.Sigmoid).then_inc(emptied[s].sem, 1)

        @block.gpsimd
        def _(pool):
            for e in (*lo_made.values(), summed, z_cos, product, h_next[0], in_sum[1]):
                e.open(pool)
            nc.gpsimd.memset(eps[:], EPS).then_inc(eps_set, 1)

            def w_low(s, l, k, kt):
                pool.wait_ge(hi_made[s].sem, hi_made[s].done(l, k))
                nc.gpsimd.tensor_tensor(w_lo[s][:, 0:kt, :].rearrange("p k n -> p (k n)"), raw[s][:, 0:kt * P],
                                        w_hi[s][:, 0:kt, :].rearrange("p k n -> p (k n)").bitcast(F32),
                                        ALU.subtract).then_inc(lo_made[s].sem, 1)

            def z_cosine(l, r):
                pool.wait_ge(z_scaled.sem, z_scaled.done(l, r))
                pool.wait_ge(z_hi.sem, z_hi.done(l, r - 2))
                pool.wait_ge(z_lo.sem, z_lo.done(l, r - 2))
                nc.gpsimd.tensor_tensor(zcos[r % 2], z[r % 3], cos_sin[:, 0, :], ALU.mult).then_inc(z_cos.sem, 1)

            with pool.Fori(0, DEPTH) as l:
                w_low("A", l, 0, KT)
                w_low("B", l, 0, KT)
                for k, t in enumerate(IN_ADDED[1]):
                    pool.wait_ge(in_sq.sem, in_sq.done(l, t))
                    pool.wait_ge(in_sum[1].sem, in_sum[1].done(l, k - 1))
                    nc.gpsimd.tensor_tensor(sum_c[:], sum_c[:], squares[1], ALU.add).then_inc(in_sum[1].sem, 1)
                pool.wait_ge(tables_in, 16)
                for g, cosines in ((2, ()), (3, (0, 1)), (4, (2,)), (5, (3,)), (6, ()), (7, (4,)), (8, ())):
                    w_low(slot_of(g)[0], l, slot_of(g)[1], KT)
                    for r in cosines:
                        z_cosine(l, r)

                pool.wait_ge(f_summed.sem, f_summed.done(l, F_IN))
                pool.sem_inc(settled["pool"], 1)
                nc.gpsimd.memset(sum_h[:], 0.0).then_inc(summed.sem, 1)

                def add_square(k, acc):
                    pool.wait_ge(squared.sem, squared.done(l, k))
                    pool.wait_ge(summed.sem, summed.done(l, k + 1))
                    nc.gpsimd.tensor_tensor(acc[:], acc[:], sq[:], ALU.add).then_inc(summed.sem, 1)

                for n in range(N_UNITS):
                    for q in ENDS[n - 1] if n else []:
                        s, k = mix_job(q + 2)
                        w_low(s, l, k, KT)
                    if n == 6:
                        pool.wait_ge(qk_placed.sem, qk_placed.done(l, 23))
                        pool.sem_inc(settled["pool"], 1)
                        nc.gpsimd.memset(sum_c[:], 0.0).then_inc(summed.sem, 1)
                    if n % 6 == 1 and n > 6:
                        add_square(2 * (n // 6 - 1), sum_h)
                    j = SQUARE_AT.get(n)
                    if j is not None:
                        add_square(2 * j + 1, sum_c)
                add_square(6, sum_h)
                s, k = mix_job(N_MIX + 1)
                w_low(s, l, k, KT)
                add_square(7, sum_c)
                w_low("A", l, AT_OUT + 1, KT)
                with pool.Fori(0, 3) as i:
                    w_low("B", l, AT_OUT + i + 1, KT)
                    w_low("A", l, AT_OUT + i + 2, KT)
                w_low("B", l, AT_UP[0], KT)

                def multiply(f, i):
                    pool.wait_ge(silued.sem, silued.done(l, f * HALF + i))
                    pool.wait_ge(up_right[1].sem, up_right[1].done(l, f * HALF + i))
                    nc.gpsimd.tensor_tensor(up_out[1], up_out[0], up_out[1], ALU.mult).then_inc(product.sem, 1)

                for f in range(HALVES):
                    with pool.Fori(0, HALF - 1) as i:
                        w_low("A", l, AT_UP[f] + i + 1, KT)
                        w_low("B", l, AT_UP[f] + i + 1, KT)
                        multiply(f, i)
                    w_low("A", l, AT_DOWN[f], HALF)
                    w_low("B", l, AT_DOWN[f], HALF)
                    multiply(f, HALF - 1)
                    with pool.Fori(0, 3) as i:
                        w_low("A", l, AT_DOWN[f] + i + 1, HALF)
                        w_low("B", l, AT_DOWN[f] + i + 1, HALF)
                    w_low("A", l, AT_DOWN[f] + 4, KT)
                    w_low("B", l, AT_DOWN[f] + 4, KT)

                for m in range(6):
                    w_low("AB"[m % 2], l, AT_PLE + m // 2 + 1, KT)
                for m in range(0, KT, 2):
                    pool.wait_ge(p_gated.sem, p_gated.done(l, m))
                    nc.gpsimd.tensor_tensor(h[:, m, :], h[:, m, :], gate[m][:], ALU.add).then_inc(h_next[0].sem, 1)

        @block.vector
        def _(dve):
            for e in (*emptied.values(), in_lo_made, f_inverted, f_lo_made, z_scaled, z_sin, z_roped, z_lo,
                      v_lo, padded, gated, left, right, mixed, topped, neg_topped, inverted, normed, pt_lo_made,
                      o_out, *scaled.values(), added, *up_left, *up_right, act_lo_made, p_lo_made, mix_lo_made, proj_lo_made, p_gated,
                      h_done, h_summed, h_next[1], in_sum[0]):
                e.open(dve)
            dve.wait_ge(spread_set, 16)
            nc.vector.tensor_copy(spread[:], zrot[0][0:F_LO.stop, :]).then_inc(spread_set, 1)
            for i in range(2):
                nc.vector.memset(f_hl[i][:].bitcast(F32), 0.0)
            def low(made, k, dst, src, hi, gain=None):
                dve.wait_ge(made[0].sem, made[0].done(*k))
                if gain is None:
                    ins = nc.vector.tensor_tensor(dst, src, hi.bitcast(F32), ALU.subtract)
                else:
                    ins = nc.vector.scalar_tensor_tensor(dst, src, gain, hi.bitcast(F32), ALU.mult, ALU.subtract)
                ins.then_inc(made[1].sem, 1)

            in_made, mix_made = (in_hi_made, in_lo_made), (mix_hi_made, mix_lo_made)

            def tile_of(t, m):
                return t[:, bass.ds(m, 1), :].rearrange("p a t -> p (a t)")

            def factor_inverse(l, f):
                dve.wait_ge(f_rooted.sem, f_rooted.done(l, f))
                if f >= 2:
                    dve.wait_ge(f_turned.sem, f_turned.done(l, f - 2))
                nc.vector.reciprocal(f_inv[f % 2][:], f_root[f % 2][:]).then_inc(f_inverted.sem, 1)

            def factor_low(l, f, bank):
                dve.wait_ge(f_hi_made.sem, f_hi_made.done(l, f))
                nc.vector.tensor_tensor(f_hl[f % 2][F_LO, :], ps[bank][0:NF, T + 16:T + 16 + P],
                                        f_hl[f % 2][F_HI, :].bitcast(F32), ALU.subtract).then_inc(f_lo_made.sem, 1)

            def add_square(l, m):
                dve.wait_ge(h_squared.sem, h_squared.done(l, m))
                dve.wait_ge(h_summed.sem, h_summed.done(l, m - 2))
                nc.vector.tensor_tensor(sum_h[:], sum_h[:], sq[:], ALU.add).then_inc(h_summed.sem, 1)

            def pads(l, k, bufs):
                ins = None
                for b in bufs:
                    for c in PADS:
                        ins = nc.vector.memset(b[:, c], 0.0)
                ins.then_inc(padded.sem, 1)

            def empty(s, l, k, out):
                dve.wait_ge(job_done[s].sem, job_done[s].done(l, k))
                if out.shape[-1] == UW:
                    nc.vector.tensor_tensor(out[:, U_PROMPT], ps[s][:, 0:SEQ], r_in[:, 0:SEQ], ALU.mult)
                    ins = nc.vector.tensor_tensor(out[:, U_SAMPLE], ps[s][:, SEQ:T], r_in[:, SEQ:T], ALU.mult)
                else:
                    ins = nc.vector.tensor_tensor(out, ps[s][:, 0:T], r_in[:], ALU.mult)
                ins.then_inc(emptied[s].sem, 1)

            def z_scale(l, r):
                dve.wait_ge(f_spread.sem, f_spread.done(l, F_HEADS + r))
                gain = V_QG if r else V_KG
                nc.vector.scalar_tensor_tensor(z[r % 3], z[r % 3], vc[:, gain:gain + 1],
                                               ps["CD"[r % 2]][:, 0:T],
                                               ALU.mult, ALU.mult).then_inc(z_scaled.sem, 1)

            def z_rope(l, r):
                dve.wait_ge(z_swapped[r % 2].sem, z_swapped[r % 2].done(l, 4 * (r // 2) + 3))
                nc.vector.tensor_tensor(zrot[r % 2], zrot[r % 2], cos_sin[:, 1, :], ALU.mult).then_inc(z_sin.sem, 1)
                dve.wait_ge(z_sin.sem, z_sin.done(l, r))
                dve.wait_ge(z_cos.sem, z_cos.done(l, r))
                nc.vector.tensor_tensor(zcos[r % 2], zcos[r % 2], zrot[r % 2], ALU.add).then_inc(z_roped.sem, 1)

            def z_low(l, r):
                dve.wait_ge(z_hi.sem, z_hi.done(l, r))
                nc.vector.tensor_tensor(qk_lo[:], zcos[r % 2], qk_hi[:].bitcast(F32), ALU.subtract).then_inc(z_lo.sem, 1)

            with dve.Fori(0, DEPTH) as l:
                dve.wait_ge(vec_set.sem, vec_set.done(l, 0))
                for t in range(KT):
                    low(in_made, (l, t), in_lo[:, t, :], h[:, t, :], in_hi[:, t, :],
                        vc[:, V_ATTN + t:V_ATTN + t + 1])
                for k, t in enumerate(IN_ADDED[0]):
                    dve.wait_ge(in_sq.sem, in_sq.done(l, t))
                    dve.wait_ge(in_sum[0].sem, in_sum[0].done(l, k - 1))
                    nc.vector.tensor_tensor(sum_h[:], sum_h[:], squares[t % 2], ALU.add).then_inc(in_sum[0].sem, 1)
                dve.wait_ge(tables_in, 16)
                factor_inverse(l, F_IN)
                factor_low(l, F_IN, "C")
                dve.wait_ge(r_copied.sem, r_copied.done(l, 0))

                def z_factor(r):
                    factor_inverse(l, F_HEADS + r)
                    factor_low(l, F_HEADS + r, "CD"[r % 2])

                def z_turn(r):
                    z_rope(l, r)
                    z_low(l, r)

                for r in range(2):
                    empty(*slot_of(r)[:1], l, slot_of(r)[1], z[r])
                for r in range(2):
                    z_factor(r)
                    z_scale(l, r)
                for r, before, after in ((2, (0,), ()), (3, (1,), ()), (4, (2,), (3,)), (5, (), ())):
                    if r >= 3:
                        dve.wait_ge(z_cos.sem, z_cos.done(l, r - 3))
                        e = z_swapped[(r - 3) % 2]
                        dve.wait_ge(e.sem, e.done(l, 4 * ((r - 3) // 2) + 3))
                    empty(*slot_of(r)[:1], l, slot_of(r)[1], z[r % 3])
                    for i in before:
                        z_turn(i)
                    if r < 5:
                        z_factor(r)
                        z_scale(l, r)
                    for i in after:
                        z_turn(i)

                def top_of(n, t, tiles):
                    nk, c = unit_of(n)[3], 2 * (n % 2) + t
                    dve.wait_ge(scored.sem, scored.done(l, 2 * n + t + tiles - 1))
                    banks = ps["C"][:, t * 512:(t + tiles) * 512].rearrange("p (t k) -> p t k", t=tiles)
                    nc.vector.reduce_max(top[:, c:c + tiles], banks[:, :, 0:nk], AX_X).then_inc(topped.sem, tiles)
                    dve.wait_ge(topped.sem, topped.done(l, 2 * n + t + tiles - 1))
                    nc.vector.tensor_scalar(neg_top[:, c:c + tiles], top[:, c:c + tiles], -SCALE, None,
                                            ALU.mult).then_inc(neg_topped.sem, tiles)

                def norm(n, t):
                    nk, c = unit_of(n)[3], 2 * (n % 2) + t
                    dve.wait_ge(exped.sem, exped.done(l, 2 * n + t))
                    nc.vector.reciprocal(inv_total[:, c:c + 1], total[:, c:c + 1]).then_inc(inverted.sem, 1)
                    dve.wait_ge(inverted.sem, inverted.done(l, 2 * n + t))
                    a = probs[:, n % 2, t, 0:nk]
                    nc.vector.tensor_scalar(a, a, inv_total[:, c:c + 1], None, ALU.mult).then_inc(normed.sem, 1)

                def pt_low(n, t, tiles):
                    nb = unit_of(n)[3] // P
                    dve.wait_ge(pt_hi_made.sem, pt_hi_made.done(l, 2 * n + t + tiles - 1))
                    lo, hi = (a[:, 0:nb, t * P:(t + tiles) * P].rearrange("p b (t q) -> p t b q", q=P)
                              for a in (pt_lo, pt_hi))
                    nc.vector.tensor_tensor(lo, both(ps["D"][:, 0:tiles * nb * P], tiles, nb), hi.bitcast(F32),
                                            ALU.subtract).then_inc(pt_lo_made.sem, tiles)

                def mixer(q):
                    (s, k), (j, part) = mix_job(q), divmod(q, 3)
                    empty(s, l, k, (conv_in, conv_out[:, 0:T], mix[:, 4 + j, :])[part])

                def mixer_gate(j):
                    for q in (3 * j, 3 * j + 1):
                        s, k = mix_job(q)
                        dve.wait_ge(emptied[s].sem, emptied[s].done(l, k))
                    nc.vector.tensor_tensor(conv_in[:, U_PROMPT], conv_in[:, U_PROMPT], conv_out[:, 0:SEQ], ALU.mult)
                    nc.vector.tensor_tensor(conv_in[:, U_SAMPLE], conv_in[:, U_SAMPLE], conv_out[:, SEQ:T],
                                            ALU.mult).then_inc(gated.sem, 1)

                def mixer_left(j):
                    dve.wait_ge(centre.sem, centre.done(l, j))
                    nc.vector.scalar_tensor_tensor(conv_out[:], conv_in[:, 0:CW], vc[:, V_MCONV + j:V_MCONV + j + 1],
                                                   conv_out[:], ALU.mult, ALU.add).then_inc(left.sem, 1)

                def mixer_right(j):
                    dve.wait_ge(left.sem, left.done(l, j))
                    c = V_MCONV + 8 + j
                    nc.vector.scalar_tensor_tensor(conv_out[:], conv_in[:, 2:2 + CW], vc[:, c:c + 1], conv_out[:],
                                                   ALU.mult, ALU.add).then_inc(right.sem, 1)

                def mixer_end(j):
                    s, k = mix_job(3 * j + 2)
                    dve.wait_ge(emptied[s].sem, emptied[s].done(l, k))
                    dve.wait_ge(right.sem, right.done(l, j))
                    gb = mix[:, 4 + j, :]
                    nc.vector.tensor_tensor(gb[:, 0:SEQ], gb[:, 0:SEQ], conv_out[:, C_PROMPT], ALU.mult)
                    nc.vector.tensor_tensor(gb[:, SEQ:T], gb[:, SEQ:T], conv_out[:, C_SAMPLE],
                                            ALU.mult).then_inc(mixed.sem, 1)

                def mixer_low(n):
                    t = MIX_ORDER[n]
                    low(mix_made, (l, n), mix_lo[:, t, :], mix[:, t, :], mix_hi[:, t, :],
                        vc[:, V_MIX + t:V_MIX + t + 1])

                mixer_steps = (mixer_gate, mixer_left, mixer_right, mixer_end)

                for t, tiles in steps_of(0):
                    top_of(0, t, tiles)
                for t in range(2):
                    norm(0, t)
                dve.wait_ge(v_hi.sem, v_hi.done(l, 0))
                nc.vector.tensor_tensor(v_hl[:, :, :, 64:128],
                                        ps["D"][:, 0:T].rearrange("p (t g d) -> p t g d", g=N_KV, d=HEAD_DIM),
                                        v_hl[:, :, :, 0:64].bitcast(F32), ALU.subtract).then_inc(v_lo.sem, 1)
                pads(l, 0, [conv_in])
                dve.wait_ge(padded.sem, padded.done(l, 0))
                mixer(0)
                for n in range(N_UNITS):
                    pt_low(n, *steps_of(n)[0])
                    if n + 1 < N_UNITS:
                        for t, tiles in steps_of(n + 1):
                            top_of(n + 1, t, tiles)
                    if unit_of(n)[3] == SEQ:
                        pt_low(n, 1, 1)
                    if n + 1 < N_UNITS:
                        norm(n + 1, 0)
                        norm(n + 1, 1)
                    if n == N_UNITS - 1:
                        mixer_low(0)
                    for q in ENDS[n - 1] if n else []:
                        mixer(q)
                    if n == 0:
                        z_rope(l, 4)
                    if n == 1:
                        z_low(l, 4)
                    for step, j in MIX_STEPS[n]:
                        mixer_steps[step](j)
                    head, q0 = unit_of(n)[:2]
                    dve.wait_ge(o_low_out.sem, o_low_out.done(l, n))
                    r = 64 * (head % 2)
                    nc.vector.tensor_tensor(mix[r:r + 64, head // 2, q0:q0 + UQ], ps["D"][0:64, 512:512 + UQ],
                                            o_low[:], ALU.add).then_inc(o_out.sem, 1)

                mixer_low(1)
                mixer_low(2)
                mixer(N_MIX - 1)
                mixer_low(3)
                mixer_low(4)
                mixer_right(3)
                mixer_end(3)
                factor_inverse(l, F_ATTN)
                mixer_low(5)
                mixer_low(6)
                factor_low(l, F_ATTN, "C")
                mixer_low(7)
                factor_inverse(l, F_CONV)
                factor_low(l, F_CONV, "D")
                t_conv, t_attn = conv_in[:, 0:T], conv_out[:, 0:T]

                def out_tile(s, k, m):
                    attn_ps, conv_ps = ("A", "B") if s == "A" else ("C", "D")
                    dve.wait_ge(job_done[s].sem, job_done[s].done(l, k))
                    dve.wait_ge(h_done.sem, h_done.done(l, m - 1))
                    nc.vector.tensor_tensor(t_attn, ps[attn_ps][:, 0:T], r_attn, ALU.mult).then_inc(
                        scaled["attn"].sem, 1)
                    if isinstance(m, int) and m == 0:
                        dve.wait_ge(r_copied.sem, r_copied.done(l, 2))
                    nc.vector.tensor_tensor(t_conv, ps[conv_ps][:, 0:T], r_conv, ALU.mult).then_inc(
                        emptied[s].sem, 1)
                    dve.wait_ge(scaled["attn"].sem, scaled["attn"].done(l, m))
                    dst = h[:, bass.ds(m, 1), :].rearrange("p a t -> p (a t)")
                    nc.vector.tensor_tensor(dst, dst, t_attn, ALU.add).then_inc(added.sem, 1)
                    dve.wait_ge(added.sem, added.done(l, m))
                    dve.wait_ge(emptied[s].sem, emptied[s].done(l, k))
                    nc.vector.tensor_tensor(dst, dst, t_conv, ALU.add).then_inc(h_done.sem, 1)
                    low(in_made, (l, KT + m), tile_of(in_lo, m), dst, tile_of(in_hi, m),
                        vc[:, bass.ds(V_FFN + m, 1)])
                    if not (isinstance(m, int) and m == 0):
                        add_square(l, m)

                dve.wait_ge(r_copied.sem, r_copied.done(l, 1))
                out_tile("A", AT_OUT, 0)
                with dve.Fori(0, 3) as i:
                    out_tile("B", AT_OUT + i, 2 * i + 1)
                    out_tile("A", AT_OUT + i + 1, 2 * i + 2)
                out_tile("B", AT_OUT + 3, 7)

                pads(l, 1, up_in)
                factor_inverse(l, F_FFN)
                factor_low(l, F_FFN, "C")

                def up_taps(f, i, side):
                    n = f * HALF + i
                    dve.wait_ge(up_centre[side].sem, up_centre[side].done(l, n))
                    c = V_FCONV + side * FF_TILES + f * HALF
                    out = up_out[side]
                    nc.vector.scalar_tensor_tensor(out, up_in[side][:, 0:CW], vc[:, bass.ds(c + i, 1)], out,
                                                   ALU.mult, ALU.add).then_inc(up_left[side].sem, 1)
                    dve.wait_ge(up_left[side].sem, up_left[side].done(l, n))
                    nc.vector.scalar_tensor_tensor(out, up_in[side][:, 2:2 + CW],
                                                   vc[:, bass.ds(c + 4 * FF_TILES + i, 1)], out,
                                                   ALU.mult, ALU.add).then_inc(up_right[side].sem, 1)

                def ffn_pair(f, i):
                    dve.wait_ge(up_right[0].sem, up_right[0].done(l, f * HALF + i - 1))
                    empty("A", l, AT_UP[f] + i, up_in[0])
                    up_taps(f, i, 0)
                    dve.wait_ge(up_right[1].sem, up_right[1].done(l, f * HALF + i - 1))
                    empty("B", l, AT_UP[f] + i, up_in[1])
                    up_taps(f, i, 1)
                    dve.wait_ge(act_hi_made.sem, act_hi_made.done(l, f * HALF + i))
                    dst = act_lo[:, bass.ds(i, 1), :].rearrange("p a c -> p (a c)")
                    hi = act_hi[:, bass.ds(i, 1), :].rearrange("p a c -> p (a c)").bitcast(F32)
                    nc.vector.tensor_tensor(dst, up_out[1], hi, ALU.subtract).then_inc(act_lo_made.sem, 1)

                def down_tile(s, k, f, m):
                    dve.wait_ge(job_done[s].sem, job_done[s].done(l, k))
                    dst = h[:, bass.ds(m, 1), :].rearrange("p a t -> p (a t)")
                    nc.vector.tensor_tensor(dst, ps[s][:, 0:T], dst, ALU.add).then_inc(h_done.sem, 1)
                    dve.wait_ge(h_done.sem, h_done.done(l, (1 + f) * KT + m))
                    emptied[s].open(dve)
                    if f == 1:
                        low(in_made, (l, 2 * KT + m), tile_of(in_lo, m), dst, tile_of(in_hi, m))

                dve.wait_ge(padded.sem, padded.done(l, 1))
                dve.wait_ge(r_copied.sem, r_copied.done(l, 3))
                dve.sem_inc(settled["dve"], 1)
                for f in range(HALVES):
                    with dve.Fori(0, HALF) as i:
                        ffn_pair(f, i)
                    with dve.Fori(0, 4) as i:
                        down_tile("A", AT_DOWN[f] + i, f, 2 * i)
                        down_tile("B", AT_DOWN[f] + i, f, 2 * i + 1)

                dve.wait_ge(p_hi_made.sem, p_hi_made.done(l, 0))
                nc.vector.tensor_tensor(p_lo[:], p_raw, p_hi[:].bitcast(F32), ALU.subtract).then_inc(p_lo_made.sem, 1)
                dve.wait_ge(proj_hi_made.sem, proj_hi_made.done(l, 0))
                nc.vector.tensor_tensor(proj_lo[:], proj_raw, proj_hi[:].bitcast(F32),
                                        ALU.subtract).then_inc(proj_lo_made.sem, 1)
                for m in range(8):
                    s, k = "AB"[m % 2], AT_PLE + m // 2
                    dve.wait_ge(emptied[s].sem, emptied[s].done(l, k))
                    dve.wait_ge(proj_done.sem, proj_done.done(l, m))
                    nc.vector.tensor_tensor(gate[m][:], ps["CD"[m % 2]][:, 0:T], gate[m][:],
                                            ALU.mult).then_inc(p_gated.sem, 1)
                    if m % 2:
                        dve.wait_ge(p_gated.sem, p_gated.done(l, m))
                        nc.vector.tensor_tensor(h[:, m, :], h[:, m, :], gate[m][:], ALU.add).then_inc(h_next[1].sem, 1)


def _weight_tiles(w, kt):
    depth, _, cols = w.shape
    a = w.reshape(depth, kt, P, cols // P, P).transpose(0, 3, 2, 1, 4)
    return a.reshape(depth * (cols // P), P, kt * P)


def _rope_tables():
    half = HEAD_DIM // 2
    freqs = np.float32(ROPE_THETA) ** (-np.arange(0, half, 2, dtype=np.float32) / np.float32(half))
    pos = np.arange(SEQ)
    row, col = (pos // GRID_W).astype(np.float32), (pos % GRID_W).astype(np.float32)
    ang = np.concatenate([row[:, None] * freqs, row[:, None] * freqs,
                          col[:, None] * freqs, col[:, None] * freqs], axis=1)
    sign = np.repeat(np.array([-1, 1, -1, 1], np.float32), HEAD_DIM // 4)
    cos, sin = np.cos(ang).T[ROPE_ORDER], (np.sin(ang) * sign).T[ROPE_ORDER]
    both = [np.tile(np.concatenate([t, t[:, :DEC_SEQ]], axis=1), (2, 1)) for t in (cos, sin)]
    return np.ascontiguousarray(np.stack(both, axis=1), dtype=np.float32)


def kernel(**inputs):
    import concourse.bacc as bacc
    from concourse.bass_utils import run_bass_kernel_spmd

    a = {k: np.asarray(v) for k, v in inputs.items()}

    def channels(prompt, sample, n):
        both = np.concatenate([prompt, sample], axis=0).T
        return both.reshape(n, P, T).transpose(1, 0, 2)

    def columns(v):
        return v.reshape(-1, P).T

    vec = []
    for l in range(DEPTH):
        vec.append(np.concatenate([columns(a["attn_norm_g"][l]), columns(a["ffn_norm_g"][l]), columns(a["attn_out_g"][l]),
                columns(a["conv_out_g"][l]), np.tile(a["q_norm_g"][l][ROPE_ORDER], 2)[:, None],
                np.tile(a["k_norm_g"][l][ROPE_ORDER], 2)[:, None], columns(a["mix_conv_w"][l]), columns(a["ffn_conv_w"][l])], axis=1))
    qk_w = ATTN_W + N_KV * HEAD_DIM
    in_order = [HEAD_DIM * head + c for head in range(qk_w // HEAD_DIM) for c in ROPE_ORDER]
    in_order += range(qk_w, D_IN)
    eye = np.eye(P, dtype=np.float32)
    halves = np.repeat(np.eye(2, dtype=np.float32), HEAD_DIM, axis=0)
    w_down = a["w_down"].reshape(DEPTH * HALVES, HALF * P, D_MODEL)
    spread = np.zeros((F_LO.stop, T), np.float32)
    spread[F_HI] = spread[F_LO] = np.kron(np.eye(T // P, dtype=np.float32), halves.T)
    arrays = {
        "x": channels(a["x_prompt"][0], a["x_sample"][0], KT),
        "p": np.stack([channels(a["p_prompt"][l, 0], a["p_sample"][l, 0], KT_PLE).reshape(P, KT_PLE * T)
                       for l in range(DEPTH)]),
        "w_in": _weight_tiles(a["w_in"][:, :, in_order], KT), "w_out": _weight_tiles(a["w_out"], KT),
        "w_up": _weight_tiles(a["w_up"], KT), "w_down": _weight_tiles(w_down, HALF),
        "w_gate": _weight_tiles(a["w_ple_gate"], KT), "w_proj": _weight_tiles(a["w_ple_proj"], KT_PLE).reshape(DEPTH, 8, P, KT_PLE * P).transpose(0, 2, 1, 3)
        .reshape(DEPTH, P, 8 * KT_PLE * P),
        "vec": np.stack(vec), "tables": _rope_tables(),
        "mats": np.concatenate([eye, np.ones((P, 2), np.float32), halves], axis=1),
        "spread": spread,
    }
    nc = bacc.Bacc("TRN2", target_bir_lowering=False, num_devices=1, dynamic_dma_scratch_size=1024)
    arrays = {f"in_{k}": np.ascontiguousarray(v) for k, v in arrays.items()}
    args = [nc.dram_tensor(k, v.shape, F32, kind="ExternalInput").ap() for k, v in arrays.items()]
    y = nc.dram_tensor("out_y", (P, KT, T), F32, kind="ExternalOutput").ap()
    trunk_program(nc, *args, y)
    r = run_bass_kernel_spmd(nc, [arrays], core_ids=[0])
    out = r.results[0]["out_y"].transpose(1, 0, 2).reshape(D_MODEL, T).T
    return (np.ascontiguousarray(out[:SEQ])[None], np.ascontiguousarray(out[SEQ:])[None])
```
